# Optimizing a Trainium2 kernel written in Bass

```python
import math
import jax
import jax.numpy as jnp
from jax import lax
import numpy as np

D_MODEL = 1024
BATCH = 1
SEQ = 512
DEPTH = 1

HEAD_DIM = 64
DIL_CONFIGS = ((128, 1), (512, 4), (2048, 16))
N_DIL_GROUPS = 3
DIL_HEADS = 4
DIL_WIDTH = DIL_HEADS * HEAD_DIM
MOBA_HEADS = 8
MOBA_WIDTH = MOBA_HEADS * HEAD_DIM
MOBA_BLOCK = 256
MOBA_TOPK = 3
MOBA_QCHUNK = 16
RMS_EPS = 1e-6
NEG_INF = -1e30
SPLIT_SIZES = (N_DIL_GROUPS * 3 * DIL_WIDTH, DIL_WIDTH, 3 * MOBA_WIDTH, MOBA_WIDTH, D_MODEL, D_MODEL)
IN_COLS = N_DIL_GROUPS * 3 * DIL_WIDTH + DIL_WIDTH + 4 * MOBA_WIDTH + 2 * D_MODEL

kernel_name = 'hybrid_dilated_moba_gated'

def alibi_slopes(n):
    return jnp.asarray(2.0 ** (-8.0 * np.arange(1, n + 1) / n), dtype=jnp.float32)

def rmsnorm(x, g):
    xf = x.astype(jnp.float32)
    y = xf * lax.rsqrt(jnp.mean(xf * xf, axis=-1, keepdims=True) + RMS_EPS)
    return (y * g.astype(jnp.float32)).astype(x.dtype)

def dilated_band_attention(q, k, v, window, dilation, slopes):
    B, S, H, Dh = q.shape
    d = dilation
    blk = window // dilation
    L = S // d
    nb = -(-L // blk)
    lp = nb * blk

    def to_res(t):
        t = t.astype(jnp.float32).reshape(B, L, d, H, Dh).transpose(0, 3, 2, 1, 4)
        t = jnp.pad(t, ((0, 0), (0, 0), (0, 0), (0, lp - L), (0, 0)))
        return t.reshape(B, H, d, nb, blk, Dh)

    def with_prev(t):
        prev = jnp.pad(t[:, :, :, :-1], ((0, 0), (0, 0), (0, 0), (1, 0), (0, 0), (0, 0)))
        return jnp.concatenate([prev, t], axis=4)

    qb = to_res(q)
    kk = with_prev(to_res(k))
    vv = with_prev(to_res(v))
    s = jnp.einsum('bhrnqd,bhrnkd->bhrnqk', qb, kk) * (Dh ** -0.5)
    qi = jnp.arange(blk)[:, None]
    kj = jnp.arange(2 * blk)[None, :]
    rel = blk + qi - kj
    blk_id = jnp.arange(nb)[:, None, None]
    valid = (rel >= 0) & (rel <= blk) & ((blk_id > 0) | (kj >= blk))
    bias = -slopes[:, None, None] * (rel * d).astype(jnp.float32)
    s = jnp.where(valid[None, None, None], s + bias[None, :, None, None], NEG_INF)
    m = jnp.max(s, axis=-1, keepdims=True)
    p = jnp.exp(s - m)
    den = jnp.sum(p, axis=-1)
    o = jnp.einsum('bhrnqk,bhrnkd->bhrnqd', p, vv) / den[..., None]
    lse = m[..., 0] + jnp.log(den)
    o = o.reshape(B, H, d, lp, Dh)[:, :, :, :L].transpose(0, 3, 2, 1, 4).reshape(B, S, H, Dh)
    lse = lse.reshape(B, H, d, lp)[:, :, :, :L].transpose(0, 3, 2, 1).reshape(B, S, H)
    return o, lse

def moba_attention(q, k, v, slopes):
    B, S, H, Dh = q.shape
    blk = MOBA_BLOCK
    nb = -(-S // blk)
    sp = nb * blk
    qc = MOBA_QCHUNK
    nch = sp // qc
    topk = min(MOBA_TOPK, nb)
    scale = Dh ** -0.5

    def prep(t):
        t = jnp.pad(t.astype(jnp.float32), ((0, 0), (0, sp - S), (0, 0), (0, 0)))
        return t.transpose(0, 2, 1, 3)

    qp, kp, vp = prep(q), prep(k), prep(v)
    kb = kp.reshape(B, H, nb, blk, Dh)
    vb = vp.reshape(B, H, nb, blk, Dh)
    kmean = jnp.mean(kb, axis=3)
    gate = jnp.einsum('bhtd,bhnd->bhtn', qp, kmean)
    qblk = jnp.arange(sp) // blk
    past = jnp.arange(nb)[None, :] < qblk[:, None]
    gate = jnp.where(past, gate, NEG_INF)
    _, sel = lax.top_k(gate, topk)
    sel_ok = sel < qblk[None, None, :, None]

    def chunks(t):
        return jnp.moveaxis(t.reshape(B, H, nch, qc, *t.shape[3:]), 2, 0)

    bidx = jnp.arange(B)[:, None, None, None]
    hidx = jnp.arange(H)[None, :, None, None]
    m = slopes[None, :, None, None]
    koff = jnp.arange(blk)

    def one_chunk(args):
        q_c, sel_c, ok_c, ci = args
        t_pos = ci * qc + jnp.arange(qc)
        c = (ci * qc) // blk
        k_sel = kb[bidx, hidx, sel_c]
        v_sel = vb[bidx, hidx, sel_c]
        s_pos = sel_c[..., None] * blk + koff
        d_sel = (t_pos[:, None, None] - s_pos).astype(jnp.float32)
        s_sel = jnp.einsum('bhqd,bhqnkd->bhqnk', q_c, k_sel) * scale - m[..., None] * d_sel
        s_sel = jnp.where(ok_c[..., None], s_sel, NEG_INF)
        k_own = lax.dynamic_index_in_dim(kb, c, axis=2, keepdims=False)
        v_own = lax.dynamic_index_in_dim(vb, c, axis=2, keepdims=False)
        d_own = t_pos[:, None] - (c * blk + koff)[None, :]
        s_own = jnp.einsum('bhqd,bhkd->bhqk', q_c, k_own) * scale - m * d_own.astype(jnp.float32)
        s_own = jnp.where(d_own >= 0, s_own, NEG_INF)
        s_all = jnp.concatenate([s_sel.reshape(B, H, qc, topk * blk), s_own], axis=-1)
        p = jax.nn.softmax(s_all, axis=-1)
        p_sel = p[..., :topk * blk].reshape(B, H, qc, topk, blk)
        p_own = p[..., topk * blk:]
        return (jnp.einsum('bhqnk,bhqnkd->bhqd', p_sel, v_sel)
                + jnp.einsum('bhqk,bhkd->bhqd', p_own, v_own))

    out = lax.map(one_chunk, (chunks(qp), chunks(sel), chunks(sel_ok), jnp.arange(nch)))
    out = jnp.moveaxis(out, 0, 2).reshape(B, H, sp, Dh)[:, :, :S]
    return out.transpose(0, 2, 1, 3)

def hybrid_layer(x, norm_g, w_in, b_merge, w_pa, w_pb, w_out):
    B, S, _ = x.shape
    h = rmsnorm(x, norm_g)
    proj = jnp.einsum('bsd,dc->bsc', h, w_in)
    offs = [int(o) for o in np.cumsum(SPLIT_SIZES)[:-1]]
    a_qkv, z_a, b_qkv, z_b, r_a, r_b = jnp.split(proj, offs, axis=-1)

    a_qkv = a_qkv.reshape(B, S, N_DIL_GROUPS, 3, DIL_HEADS, HEAD_DIM)
    slopes_a = alibi_slopes(N_DIL_GROUPS * DIL_HEADS).reshape(N_DIL_GROUPS, DIL_HEADS)
    outs, lses = [], []
    for g, (window, dilation) in enumerate(DIL_CONFIGS):
        o, lse = dilated_band_attention(a_qkv[:, :, g, 0], a_qkv[:, :, g, 1], a_qkv[:, :, g, 2],
                                        window, dilation, slopes_a[g])
        outs.append(o)
        lses.append(lse)
    wts = jax.nn.softmax(jnp.stack(lses, axis=0), axis=0)
    attn_a = jnp.sum(wts[..., None] * jnp.stack(outs, axis=0), axis=0).reshape(B, S, DIL_WIDTH)
    y_a = jnp.einsum('bsc,cd->bsd', attn_a.astype(x.dtype) * jax.nn.silu(z_a), w_pa)

    b_qkv = b_qkv.reshape(B, S, 3, MOBA_HEADS, HEAD_DIM)
    attn_b = moba_attention(b_qkv[:, :, 0], b_qkv[:, :, 1], b_qkv[:, :, 2],
                            alibi_slopes(MOBA_HEADS)).reshape(B, S, MOBA_WIDTH)
    y_b = jnp.einsum('bsc,cd->bsd', attn_b.astype(x.dtype) * jax.nn.silu(z_b), w_pb)

    merged = (jax.nn.sigmoid(r_a + b_merge[:D_MODEL]) * y_a
              + jax.nn.sigmoid(r_b + b_merge[D_MODEL:]) * y_b)
    return x + jnp.einsum('bsd,de->bse', merged, w_out)

def setup_inputs(seed: int = 0) -> dict:
    key = jax.random.key(seed)
    ks = jax.random.split(key, 8)
    x = jax.random.normal(ks[0], (BATCH, SEQ, D_MODEL), jnp.float32)
    norm_g = 1.0 + 0.05 * jax.random.normal(ks[1], (DEPTH, D_MODEL), jnp.float32)
    w_in = jax.random.normal(ks[2], (DEPTH, D_MODEL, IN_COLS), jnp.float32) * D_MODEL ** -0.5
    b_merge = 0.1 * jax.random.normal(ks[3], (DEPTH, 2 * D_MODEL), jnp.float32)
    w_pa = jax.random.normal(ks[4], (DEPTH, DIL_WIDTH, D_MODEL), jnp.float32) * DIL_WIDTH ** -0.5
    w_pb = jax.random.normal(ks[5], (DEPTH, MOBA_WIDTH, D_MODEL), jnp.float32) * MOBA_WIDTH ** -0.5
    w_out = jax.random.normal(ks[6], (DEPTH, D_MODEL, D_MODEL), jnp.float32) * D_MODEL ** -0.5
    final_g = 1.0 + 0.05 * jax.random.normal(ks[7], (D_MODEL,), jnp.float32)
    return {'x': x, 'norm_g': norm_g, 'w_in': w_in, 'b_merge': b_merge,
            'w_pa': w_pa, 'w_pb': w_pb, 'w_out': w_out, 'final_g': final_g}

def reference(x, norm_g, w_in, b_merge, w_pa, w_pb, w_out, final_g):
    for layer in range(DEPTH):
        x = hybrid_layer(x, norm_g[layer], w_in[layer], b_merge[layer],
                         w_pa[layer], w_pb[layer], w_out[layer])
    return rmsnorm(x, final_g)


_drawn_inputs = setup_inputs


def setup_inputs(seed=0):
    import zlib

    import numpy as np

    out = dict(_drawn_inputs(seed))
    spreads = {}
    factors = {'norm_g': 3.942, 'b_merge': 8.0}
    for name, (base, spread) in spreads.items():
        noise = np.random.default_rng([zlib.crc32(name.encode()), seed]).standard_normal(out[name].shape)
        drawn = base * np.exp(spread * noise) if base else spread * noise
        out[name] = jnp.asarray(drawn.astype(out[name].dtype))
    for name, factor in factors.items():
        out[name] = (out[name] * factor).astype(out[name].dtype)
    return out
```

```python
from contextlib import ExitStack

import concourse.bass as bass
from concourse import mybir
import numpy as np

F32 = mybir.dt.float32
F32R = mybir.dt.float32r
ALU = mybir.AluOpType
ACT = mybir.ActivationFunctionType
AX = mybir.AxisListType

P = 128
SEQ = 512
D = 1024
TT = SEQ // P
KT_D = D // P
HD = 64
HU = 4
UW = HU * HD
EPS = 1e-6
BIG = 1e32

BAND, QUAD, HEX, FULL = range(4)
UNITS = [BAND, QUAD, HEX, FULL, FULL]
NU = len(UNITS)
NH = NU * HU
NDIL = 3
DIL = [1, 4, 16]
C_A = NDIL * 3 * UW
C_ZA = C_A
C_B = C_ZA + UW
C_ZB = C_B + 3 * 2 * UW
C_RA = C_ZB + 2 * UW
C_RB = C_RA + D


def slopes(n):
    return [float(np.float32(2.0 ** (-8.0 * (i + 1) / n))) for i in range(n)]


SLOPE = slopes(NDIL * HU) + slopes(2 * HU)

CHUNKS = []
for u, kind in enumerate(UNITS):
    q = u * 3 * UW if u < NDIL else C_B + (u - NDIL) * UW
    w = UW if u < NDIL else 2 * UW
    CHUNKS += [("k", q + w), ("q", q), ("v", q + 2 * w)]
CHUNKS += [("z", C_ZA), ("z", C_ZB), ("z", C_ZB + UW)]
NZ0 = 2 * 3 * NU
NR0 = NZ0 + 6
ND = D // P
for j in range(ND // 2):
    CHUNKS += [("ra", C_RA + 256 * j), ("rb", C_RB + 256 * j), ("y", 256 * j)]
NS = 2 * len(CHUNKS)
OUT_AT = len(CHUNKS) - 3
LOADS = [("w", c) for c in range(OUT_AT)] + [("out", 0), ("out", 1)] + \
        [("w", c) for c in range(OUT_AT, len(CHUNKS))] + [("out", 2), ("out", 3)]
NRAW = 3
NRING = 3
LOAD_OF = {item: n for n, item in enumerate(LOADS)}


def step_kind(n):
    return CHUNKS[n // 2][0]


def pbank(n):
    return n % 2


def puse(n):
    return sum(1 for m in range(n) if m % 2 == n % 2 and step_kind(m) != "y")


def ysteps(n):
    return sum(1 for m in range(n) if step_kind(m) == "y")


def fills(kind):
    if kind == FULL:
        return [(0, P * (i + 1), [(i, 0, 0, P * (i + 1))]) for i in range(TT)]
    if kind == BAND:
        return [(P, 512, [(0, P, 0, P), (1, 256, 0, 256)]),
                (0, 512, [(2, 0, P, 256), (3, 256, 2 * P, 256)])]
    return [(0, 512, [(i, P * i, P * i, P) for i in range(TT)])]


def prow(kind):
    if kind == FULL:
        return [(P * i * (i + 1) // 2, P * (i + 1)) for i in range(TT)]
    if kind == BAND:
        return [(P, P), (256, 256), (512, 256), (768, 256)]
    return [(P * i, P) for i in range(TT)]


def pfill(kind, f):
    if kind == FULL:
        return P * f * (f + 1) // 2
    return 512 * f


def blocks(kind):
    out = []
    for i, (at, n) in enumerate(prow(kind)):
        for b in range(n // P):
            kt = b if kind == FULL else (i - n // P + 1 + b if kind == BAND else i)
            out.append((i, kt, at + P * b))
    return out


def minima(kind):
    if kind == FULL:
        return [(i, 1, i) for i in range(TT)]
    if kind == BAND:
        return [(0, 1, 0), (1, 1, 0), (2, 2, 1)]
    return [(0, TT, 0)]


class Head:
    pass


HEADS = []
_s = _m = _t = 0
for h in range(NH):
    x = Head()
    x.n, x.unit, x.kind = h, h // HU, UNITS[h // HU]
    x.local, x.pair, x.part = h % HU, (h % HU) // 2, HD * (h % 2)
    x.fills, x.rows, x.blocks, x.minima = fills(x.kind), prow(x.kind), blocks(x.kind), minima(x.kind)
    x.s0, x.m0, x.t0 = _s, _m, _t
    x.tfills = -(-len(x.blocks) // 4)
    _s, _m, _t = _s + len(x.fills), _m + len(x.minima), _t + x.tfills
    HEADS.append(x)


def scores_slot(h):
    return 6 * (h // HU + 1) + h % HU


SCORES = {scores_slot(h): h for h in range(NH)}
TURNS = {scores_slot(h) + 1: h for h in range(NH)}
VALUES = {scores_slot(h) + 2: h for h in range(NH)}

MISC = []
for u in range(NU):
    MISC += [(6 * u + 5, "v", (u, 0)), (6 * u + 6, "v", (u, 1))]
COEF = scores_slot(NDIL * HU - 1) + 3
MISC += [(COEF + 2, "a", (0, 0)), (COEF + 3, "a", (0, 1)), (COEF + 4, "a", (0, 2)),
         (COEF + 7, "a", (1, 0)), (COEF + 8, "a", (1, 1)), (COEF + 9, "a", (1, 2))]
MISC += [(NZ0 + 3 + c, "b", c) for c in range(4)]
MISC.sort(key=lambda m: m[0])
GATED_A = {NZ0 + 3: 0, NZ0 + 4: 1}
GATED_B = {NZ0 + 3 + c: c for c in range(4)}
GATED = [("a", 0), ("b", 0), ("a", 1), ("b", 1), ("b", 2), ("b", 3)]
assert COEF + 9 <= NZ0 + 3


def gated_in(slot):
    return [n for n, (w, c) in enumerate(GATED)
            if (GATED_A if w == "a" else GATED_B).get(slot) == c]


def hybrid_layer_program(nc, x, norm_g, w_in, b_merge, w_pa, w_pb, w_out, final_g, out):
    stats_dram = nc.dram_tensor("stats_by_position", (SEQ, NDIL * 8), F32, kind="Internal").ap()
    top = ExitStack()
    with top:
        def sb(name, shape, dt, stack=top):
            return stack.enter_context(nc.sbuf_tensor(name, shape, dt))

        def sem(name):
            return top.enter_context(nc.semaphore(name))

        raw = sb("raw", [P, NRAW, 2048], F32)
        w_hi = sb("w_hi", [P, NRING, 1024], F32R)
        w_lo = sb("w_lo", [P, NRING, 1024], F32R)
        gat_hi = sb("gat_hi", [P, 6, SEQ], F32R)
        gat_lo = sb("gat_lo", [P, 6, SEQ], F32R)
        fg = sb("fg", [P, D], F32)
        d_full = sb("d_full", [P, 512], F32)
        d_band = sb("d_band", [P, 512], F32)
        d_quad = sb("d_quad", [P, P], F32)
        d_hex = sb("d_hex", [P, P], F32)
        ident = sb("ident", [P, P], F32)
        vecs = sb("vecs", [24, P], F32)
        gb = sb("gb", [P, 24], F32)
        hbias = sb("hbias", [P, 16], F32)
        ss = sb("ss", [P, 16], F32)
        var = sb("var", [P, 8], F32)
        rvar = sb("rvar", [P, 8], F32)
        rstd = sb("rstd", [P, 8], F32)

        hstack = ExitStack()
        hT_hi = sb("hT_hi", [P, KT_D, SEQ], F32R, hstack)
        hT_lo = sb("hT_lo", [P, KT_D, SEQ], F32R, hstack)
        xstack = ExitStack()
        xs = sb("xs", [P, TT, D], F32, xstack)
        squares = sb("squares", [P, TT, D], F32, xstack)
        xstack.close()
        astack = ExitStack()
        probs = sb("probs", [P, 2, 1280], F32, astack)
        KTs = sb("KTs", [P, 2, 2, SEQ], F32, astack)
        QTs = sb("QTs", [P, 2, 2, SEQ], F32, astack)
        VTs = sb("VTs", [P, 2, SEQ], F32, astack)
        Vs = sb("Vs", [P, 2, TT, UW], F32, astack)
        probsT = sb("probsT", [P, 2, 1280], F32, astack)
        o_dil = sb("o_dil", [P, NDIL, TT, UW], F32, astack)
        o_full = sb("o_full", [P, TT, 2 * UW], F32, astack)
        zf = sb("zf", [P, 6, SEQ], F32, astack)
        dil_T = sb("dil_T", [P, 2, SEQ], F32, astack)
        stats = sb("stats", [P, TT, NDIL * 8], F32, astack)
        stats3 = sb("stats3", [P, NDIL * TT, NDIL, 8], F32, astack)
        gmin = sb("gmin", [P, NDIL * TT, HU], F32, astack)
        gdif = sb("gdif", [P, NDIL * TT, NDIL, HU], F32, astack)
        gexp = sb("gexp", [P, NDIL * TT, NDIL, HU], F32, astack)
        gsum = sb("gsum", [P, NDIL * TT, NDIL, HU], F32, astack)
        gtot = sb("gtot", [P, NDIL * TT, HU], F32, astack)
        grec = sb("grec", [P, NDIL * TT, HU], F32, astack)
        coef = sb("coef", [P, NDIL * TT, HU], F32, astack)
        fmin = sb("fmin", [P, 2 * HU, TT], F32, astack)
        fsum = sb("fsum", [P, 2 * HU, TT], F32, astack)
        frec = sb("frec", [P, 2 * HU, TT], F32, astack)
        astack.close()
        hstack.close()
        wo_b_hi = sb("wo_b_hi", [P, 3, D], F32R)
        wo_b_lo = sb("wo_b_lo", [P, 3, D], F32R)
        res = sb("res", [P, 2, D], F32)
        gate = sb("gate", [P, 4, SEQ], F32)
        wo_a_hi = sb("wo_a_hi", [P, 5, D], F32R)
        wo_a_lo = sb("wo_a_lo", [P, 5, D], F32R)
        mrg_hi = sb("mrg_hi", [P, ND, SEQ], F32R)
        mrg_lo = sb("mrg_lo", [P, ND, SEQ], F32R)
        ysum = sb("ysum", [P, 2, SEQ], F32)

        ps = top.enter_context(nc.psum_tensor("ps", [P, 8, 512], F32))
        SB, TB, PVB, MB = 2, 4, 6, 7
        OUT_BANKS = [4, 5, 0, 1, 6, 7, 2, 3]

        x_in = [sem(f"x_in{i}") for i in range(TT)]
        vec_in = sem("vec_in")
        fg_in = sem("fg_in")
        raw_in = [sem(f"raw_in{i}") for i in range(NRAW)]
        const_step = sem("const_step")
        consts_ready = sem("consts_ready")
        squared = sem("squared")
        act_chain = sem("act_chain")
        dve_chain = sem("dve_chain")
        var_ready = sem("var_ready")
        rstd_ready = sem("rstd_ready")
        x_scaled = sem("x_scaled")
        vecs_turned = sem("vecs_turned")
        gb_ready = sem("gb_ready")
        x_turned = sem("x_turned")
        hT_hi_ready = sem("hT_hi_ready")
        hT_lo_ready = sem("hT_lo_ready")
        hi_ready = sem("hi_ready")
        lo_ready = sem("lo_ready")
        wo_hi_ready = sem("wo_hi_ready")
        wo_lo_ready = sem("wo_lo_ready")
        projected = sem("projected")
        proj_taken = [sem(f"proj_taken{b}") for b in range(2)]
        z_tanh = sem("z_tanh")
        misc_ready = sem("misc_ready")
        misc_taken = sem("misc_taken")
        scored = sem("scored")
        masked = sem("masked")
        min_ready = sem("min_ready")
        exp_ready = sem("exp_ready")
        turned = sem("turned")
        turn_taken = [sem(f"turn_taken{b}") for b in range(2)]
        valued = sem("valued")
        values_taken = sem("values_taken")
        stats_out = sem("stats_out")
        stats_in = sem("stats_in")
        gdif_ready = sem("gdif_ready")
        gexp_ready = sem("gexp_ready")
        o_scaled = sem("o_scaled")
        dil_gated = sem("dil_gated")
        gated_hi = sem("gated_hi")
        gated_lo = sem("gated_lo")
        y_taken = sem("y_taken")
        merged = sem("merged")
        mrg_hi_ready = sem("mrg_hi_ready")
        mrg_lo_ready = sem("mrg_lo_ready")
        out_ready = sem("out_ready")
        res_in = [sem(f"res_in{i}") for i in range(2)]
        res_added = sem("res_added")
        res_squared = sem("res_squared")
        out_var = sem("out_var")
        out_rstd = sem("out_rstd")
        out_done = sem("out_done")
        stored = [sem(f"stored{i}") for i in range(2)]

        w_in_t = w_in.rearrange("(k p) c -> p k c", p=P)
        w_pa_t = w_pa.rearrange("(k p) c -> p k c", p=P)
        w_pb_t = w_pb.rearrange("(k p) c -> p k c", p=P)
        w_out_t = w_out.rearrange("(k p) c -> p k c", p=P)
        x_t = x.rearrange("b (n p) d -> p (b n) d", p=P)
        out_t = out.rearrange("b (n p) d -> p (b n) d", p=P)

        def raw_waits(item):
            n = LOAD_OF[item]
            count = 0
            for m in range(n % NRAW, n + 1, NRAW):
                k, c = LOADS[m]
                count += 32 if k == "w" and CHUNKS[c][0] == "y" else 16
            return raw_in[n % NRAW], count

        def halves_before(n):
            return (2 * sum(1 for k, _ in LOADS[:n + 1] if k == "w"),
                    2 * sum(1 for k, _ in LOADS[:n + 1] if k == "out"))

        def raw_half(n):
            slot = LOAD_OF[("w", n // 2)] % NRAW
            kt = 6 if step_kind(n) == "y" else KT_D
            return raw[:, slot, 0:kt * 256].rearrange("p (k c) -> p k c", k=kt)[:, :, P * (n % 2):P * (n % 2) + P], kt

        def ring(t, n, kt):
            return t[:, n % NRING, 0:kt * P].rearrange("p (k c) -> p k c", k=kt)

        def raw_out(k):
            return raw[:, LOAD_OF[("out", k // 2)] % NRAW, D * (k % 2):D * (k % 2) + D]

        def wo(part, k):
            a, b = (wo_a_hi, wo_b_hi) if part == "hi" else (wo_a_lo, wo_b_lo)
            return a[:, k, :] if k < 5 else b[:, k - 5, :]

        def residue_order(kind, t):
            return t if kind in (BAND, FULL) else t.rearrange("p (i r) -> p r i", r=DIL[kind])

        def residue_major(kind, t):
            return t if kind in (BAND, FULL) else t.rearrange("p (r i) -> p r i", r=DIL[kind])

        def nmin(h, i, n=1):
            if h.unit < NDIL:
                return stats[:, i:i + n, 8 * h.unit + h.local]
            return fmin[:, h.n - NDIL * HU, i:i + n]

        def psum_den(h, i):
            if h.unit < NDIL:
                return stats[:, i, 8 * h.unit + HU + h.local:8 * h.unit + HU + h.local + 1]
            return fsum[:, h.n - NDIL * HU, i:i + 1]

        def turn_taken_wait(eng, fill):
            eng.wait_ge(turn_taken[fill % 2], fill // 2 + 1)

        def proj_taken_wait(eng, n):
            eng.wait_ge(proj_taken[pbank(n)], puse(n) + 1)

        block = top.enter_context(nc.Block())

        @block.sync
        def _(sp):
            for i in range(TT):
                sp.dma_start(xs[:, i, :], x_t[:, i, :]).then_inc(x_in[i], 16)
            sp.dma_start(vecs[0:8, :], norm_g.rearrange("l (k p) -> (l k) p", p=P)).then_inc(vec_in, 16)
            sp.dma_start(vecs[8:24, :], b_merge.rearrange("l (k p) -> (l k) p", p=P)).then_inc(vec_in, 16)
            for n, (k, c) in enumerate(LOADS):
                if n >= NRAW:
                    ring_n, out_n = halves_before(n - NRAW)
                    sp.wait_ge(hi_ready, ring_n)
                    sp.wait_ge(lo_ready, ring_n)
                    if out_n:
                        sp.wait_ge(wo_hi_ready, out_n)
                        sp.wait_ge(wo_lo_ready, out_n)
                slot, s = raw[:, n % NRAW, :], raw_in[n % NRAW]
                if k == "out":
                    sp.dma_start(slot.rearrange("p (k c) -> p k c", k=2), w_out_t[:, 2 * c:2 * c + 2, :]).then_inc(s, 16)
                elif CHUNKS[c][0] == "y":
                    at = CHUNKS[c][1]
                    dst = slot[:, 0:6 * 256].rearrange("p (k c) -> p k c", k=6)
                    sp.dma_start(dst[:, 0:2, :], w_pa_t[:, :, at:at + 256]).then_inc(s, 16)
                    sp.dma_start(dst[:, 2:6, :], w_pb_t[:, :, at:at + 256]).then_inc(s, 16)
                else:
                    at = CHUNKS[c][1]
                    sp.dma_start(slot.rearrange("p (k c) -> p k c", k=KT_D), w_in_t[:, :, at:at + 256]).then_inc(s, 16)
                if n == 3:
                    sp.dma_start(fg[:, :], final_g.partition_broadcast(P)).then_inc(fg_in, 16)
            sp.wait_ge(projected, NS - 2)
            for i in range(2):
                sp.dma_start(res[:, i, :], x_t[:, i, :]).then_inc(res_in[i], 16)
            for i in range(TT):
                sp.wait_ge(out_done, i + 1)
                sp.dma_start(out_t[:, i, :], res[:, i % 2, :]).then_inc(stored[i % 2], 16)
                if i + 2 < TT:
                    sp.wait_ge(stored[i % 2], 16)
                    sp.dma_start(res[:, i % 2, :], x_t[:, i + 2, :]).then_inc(res_in[i % 2], 16)
            for i in range(2):
                sp.wait_ge(stored[i], 32)

        @block.gpsimd
        def _(pool):
            steps = [0]

            def link(ins):
                ins.then_inc(const_step, 1)
                steps[0] += 1
                pool.wait_ge(const_step, steps[0])

            link(nc.gpsimd.memset(ident[:], 0.0))
            nc.gpsimd.affine_select(out=ident[:], in_=ident[:], compare_op=ALU.not_equal, fill=1.0, base=0,
                                    pattern=[[-1, P]], channel_multiplier=1).then_inc(consts_ready, 1)
            pool.wait_ge(consts_ready, 1)

            def lows(n):
                pool.wait_ge(hi_ready, n + 1)
                s, count = raw_waits(("w", n // 2))
                pool.wait_ge(s, count)
                if n >= NRING:
                    pool.wait_ge(projected, n - NRING + 1)
                src, kt = raw_half(n)
                nc.gpsimd.tensor_tensor(ring(w_lo, n, kt), src, ring(w_hi, n, kt).bitcast(F32),
                                        ALU.subtract).then_inc(lo_ready, 1)

            lows(0)
            link(nc.gpsimd.iota(d_full[:], [[-1, 512]], base=384, channel_multiplier=1,
                                allow_small_or_imprecise_dtypes=True))
            link(nc.gpsimd.affine_select(out=d_full[:], in_=d_full[:], compare_op=ALU.is_ge, fill=BIG, base=384,
                                         pattern=[[-1, 512]], channel_multiplier=1))
            lows(1)
            band = d_band[:].rearrange("p (a c) -> p a c", a=2)
            link(nc.gpsimd.iota(band, [[0, 2], [-1, 256]], base=P, channel_multiplier=1,
                                allow_small_or_imprecise_dtypes=True))
            link(nc.gpsimd.affine_select(out=band, in_=band, compare_op=ALU.is_ge, fill=BIG, base=P,
                                         pattern=[[0, 2], [-1, 256]], channel_multiplier=1))
            link(nc.gpsimd.affine_select(out=band, in_=band, compare_op=ALU.is_ge, fill=BIG, base=0,
                                         pattern=[[0, 2], [1, 256]], channel_multiplier=-1))
            link(nc.gpsimd.iota(d_quad[:], [[-4, P]], base=0, channel_multiplier=4,
                                allow_small_or_imprecise_dtypes=True))
            link(nc.gpsimd.affine_select(out=d_quad[:], in_=d_quad[:], compare_op=ALU.is_ge, fill=BIG, base=0,
                                         pattern=[[-1, P]], channel_multiplier=1))
            link(nc.gpsimd.memset(d_hex[:], BIG))
            for r in range(4):
                b = d_hex[32 * r:32 * r + 32, 32 * r:32 * r + 32]
                link(nc.gpsimd.iota(b, [[-16, 32]], base=0, channel_multiplier=16,
                                    allow_small_or_imprecise_dtypes=True))
                last = nc.gpsimd.affine_select(out=b, in_=b, compare_op=ALU.is_ge, fill=BIG, base=0,
                                               pattern=[[-1, 32]], channel_multiplier=1)
                if r < 3:
                    link(last)
            last.then_inc(consts_ready, 1)
            pool.wait_ge(consts_ready, 2)
            for n in range(2, NS):
                lows(n)

        @block.tensor
        def _(pe):
            pe.wait_ge(consts_ready, 1)
            pe.wait_ge(vec_in, 32)
            pe.transpose(ps[:, 7, 0:24], vecs[:, :], ident[0:24, 0:24]).then_inc(vecs_turned, 1)
            for i in range(TT):
                pe.wait_ge(x_scaled, i + 1)
                if i == 0:
                    pe.wait_ge(gb_ready, 1)
                for k in range(KT_D):
                    last = pe.transpose(ps[:, k, P * i:P * i + P], xs[:, i, P * k:P * k + P], ident[:, :])
                last.then_inc(x_turned, 1)

            def products(bank, kts, wh, wl, hh, hl, k0=0):
                for k in range(kts):
                    if hh is hT_hi and waits_hT[0] <= k:
                        pe.wait_ge(hT_lo_ready, k + 1)
                        waits_hT[0] = k + 1
                    pe.matmul(ps[:, bank, :], wh[:, k, :], hh[:, k0 + k, :], start=(k == 0), stop=False)
                    pe.matmul(ps[:, bank, :], wh[:, k, :], hl[:, k0 + k, :], start=False, stop=False)
                    last = pe.matmul(ps[:, bank, :], wl[:, k, :], hh[:, k0 + k, :], start=False, stop=(k == kts - 1))
                return last

            waits_hT = [0]

            def step(n):
                pe.wait_ge(hi_ready, n + 1)
                pe.wait_ge(lo_ready, n + 1)
                if step_kind(n) == "y":
                    if n == NR0 + 4:
                        pe.wait_ge(gated_hi, 6)
                        pe.wait_ge(gated_lo, 6)
                        pe.wait_ge(masked, _s)
                    if ysteps(n):
                        pe.wait_ge(y_taken, ysteps(n))
                    wh, wl = ring(w_hi, n, 6), ring(w_lo, n, 6)
                    products(SB, 2, wh[:, 0:2, :], wl[:, 0:2, :], gat_hi, gat_lo)
                    last = products(SB + 1, 4, wh[:, 2:6, :], wl[:, 2:6, :], gat_hi, gat_lo, 2)
                else:
                    if n < 2:
                        pe.wait_ge(hT_lo_ready, n + 1)
                        waits_hT[0] = max(waits_hT[0], n + 1)
                    if puse(n):
                        pe.wait_ge(proj_taken[pbank(n)], puse(n))
                    last = products(pbank(n), KT_D, ring(w_hi, n, KT_D), ring(w_lo, n, KT_D), hT_hi, hT_lo)
                last.then_inc(projected, 1)

            def turn_misc(m, what, at):
                if m:
                    pe.wait_ge(misc_taken, m)
                if what == "v":
                    u, j = at
                    proj_taken_wait(pe, 6 * u + 4 + j)
                    src = [VTs[:, j, P * t:P * t + P] for t in range(TT)]
                elif what == "a":
                    c, g = at
                    pe.wait_ge(o_scaled, g + 1)
                    src = [o_dil[:, g, t, P * c:P * c + P] for t in range(TT)]
                else:
                    pe.wait_ge(values_taken, NDIL * HU + 2 * at + 2)
                    src = [o_full[:, t, P * at:P * at + P] for t in range(TT)]
                for t in range(TT):
                    last = pe.transpose(ps[:, MB, P * t:P * t + P], src[t], ident[:, :])
                last.then_inc(misc_ready, 1)

            def scores(h):
                u = h.unit
                proj_taken_wait(pe, 6 * u + h.pair)
                proj_taken_wait(pe, 6 * u + 2 + h.pair)
                K, Q = (t[h.part:h.part + HD, u % 2, h.pair, :] for t in (KTs, QTs))
                for f, (_, _, tiles) in enumerate(h.fills):
                    if h.s0 + f >= 2:
                        pe.wait_ge(masked, h.s0 + f - 1)
                    for i, at, k0, nk in tiles:
                        last = pe.matmul(ps[:, SB + (h.s0 + f) % 2, at:at + nk], Q[:, P * i:P * i + P],
                                         K[:, k0:k0 + nk], start=True, stop=True)
                    last.then_inc(scored, 1)

            def turns(h):
                for f in range(h.tfills):
                    if h.t0 + f >= 2:
                        turn_taken_wait(pe, h.t0 + f - 2)
                    for b, (i, _, at) in enumerate(h.blocks[4 * f:4 * f + 4]):
                        pe.wait_ge(exp_ready, TT * h.n + i + 1)
                        last = pe.transpose(ps[:, TB + (h.t0 + f) % 2, P * b:P * b + P],
                                            probs[:, h.n % 2, at:at + P], ident[:, :])
                    last.then_inc(turned, 1)

            def values(h):
                for f in range(h.tfills):
                    turn_taken_wait(pe, h.t0 + f)
                if h.n:
                    pe.wait_ge(values_taken, h.n)
                m = [w == "v" and at == (h.unit, h.pair) for _, w, at in MISC].index(True)
                pe.wait_ge(misc_taken, m + 1)
                for i in range(TT):
                    mine = [(b, kt) for b, (q, kt, _) in enumerate(h.blocks) if q == i]
                    for b, kt in mine:
                        last = pe.matmul(ps[:, PVB, HD * i:HD * i + HD], probsT[:, h.n % 2, P * b:P * b + P],
                                         Vs[:, h.unit % 2, kt, HD * h.local:HD * h.local + HD],
                                         start=((b, kt) == mine[0]), stop=((b, kt) == mine[-1]))
                last.then_inc(valued, 1)

            for s in range(NS):
                step(s)
                for m, (slot, what, at) in enumerate(MISC):
                    if slot == s:
                        turn_misc(m, what, at)
                if s in TURNS:
                    turns(HEADS[TURNS[s]])
                if s in SCORES:
                    scores(HEADS[SCORES[s]])
                if s in VALUES:
                    values(HEADS[VALUES[s]])

            for i in range(TT):
                banks = [OUT_BANKS[2 * i], OUT_BANKS[2 * i + 1]]
                if 2 in banks:
                    pe.wait_ge(y_taken, ysteps(NS))
                if 0 in banks:
                    proj_taken_wait(pe, NS - 3)
                    proj_taken_wait(pe, NS - 4)
                if MB in banks:
                    pe.wait_ge(misc_taken, len(MISC))
                    pe.wait_ge(values_taken, NH)
                if TB in banks:
                    for b in range(2):
                        turn_taken_wait(pe, _t - 1 - b)
                order = [(k, e) for k in range(KT_D) for e in range(2)] if i == 0 else \
                        [(k, e) for e in range(2) for k in range(KT_D)]
                for k, e in order:
                    if i == 0 and e == 0:
                        pe.wait_ge(wo_lo_ready, k + 1)
                        pe.wait_ge(wo_hi_ready, k + 1)
                        pe.wait_ge(mrg_hi_ready, k + 1)
                        pe.wait_ge(mrg_lo_ready, k + 1)
                    o, cols = ps[:, banks[e], :], slice(512 * e, 512 * e + 512)
                    mh, ml = mrg_hi[:, k, P * i:P * i + P], mrg_lo[:, k, P * i:P * i + P]
                    pe.matmul(o, mh, wo("hi", k)[:, cols], start=(k == 0), stop=False)
                    pe.matmul(o, mh, wo("lo", k)[:, cols], start=False, stop=False)
                    last = pe.matmul(o, ml, wo("hi", k)[:, cols], start=False, stop=(k == KT_D - 1))
                    if k == KT_D - 1:
                        last.then_inc(out_ready, 1)

        @block.scalar
        def _(act):
            def highs(n):
                s, count = raw_waits(("w", n // 2))
                act.wait_ge(s, count)
                if n >= NRING:
                    act.wait_ge(projected, n - NRING + 1)
                    act.wait_ge(lo_ready, n - NRING + 1)
                src, kt = raw_half(n)
                nc.scalar.copy(ring(w_hi, n, kt), src).then_inc(hi_ready, 1)

            def wo_highs(k):
                s, count = raw_waits(("out", k // 2))
                act.wait_ge(s, count)
                if k == 0:
                    act.wait_ge(gated_lo, 6)
                    act.wait_ge(gated_hi, 6)
                if k == 5:
                    act.wait_ge(projected, NS - 2)
                nc.scalar.copy(wo("hi", k), raw_out(k)).then_inc(wo_hi_ready, 1)

            for i in range(TT):
                act.wait_ge(x_in[i], 16)
                nc.scalar.activation(squares[:, i, :], xs[:, i, :], ACT.Square,
                                     accum_out=ss[:, i:i + 1]).then_inc(squared, 1)
                if i:
                    act.wait_ge(var_ready, i)
                    nc.scalar.activation(rstd[:, i - 1:i], rvar[:, i - 1:i], ACT.Sqrt).then_inc(rstd_ready, 1)
            act.wait_ge(var_ready, TT)
            nc.scalar.activation(rstd[:, TT - 1:TT], rvar[:, TT - 1:TT], ACT.Sqrt).then_inc(rstd_ready, 1)
            highs(0)
            act.wait_ge(x_turned, TT)
            act.wait_ge(gb_ready, 1)
            for k in range(KT_D):
                nc.scalar.activation(hT_hi[:, k, :], ps[:, k, :], ACT.Copy,
                                     scale=gb[:, k:k + 1]).then_inc(hT_hi_ready, 1)
                if k == 4:
                    highs(1)

            def take_step(n):
                kind = step_kind(n)
                u, j = n // 6, n % 2
                src = ps[:, pbank(n), :]
                if kind in ("q", "v"):
                    act.wait_ge(projected, n + 1)
                    if kind == "q":
                        if u >= 2:
                            act.wait_ge(scored, HEADS[HU * (u - 1)].s0)
                        dst = QTs[:, u % 2, j, :]
                    else:
                        if u:
                            m = [w == "v" and at == (u - 1, j) for _, w, at in MISC].index(True)
                            act.wait_ge(misc_ready, m + 1)
                        dst = VTs[:, j, :]
                    nc.scalar.activation(residue_major(UNITS[u], dst), residue_order(UNITS[u], src), ACT.Copy,
                                         scale=HD ** -0.5 if kind == "q" else 1.0).then_inc(proj_taken[pbank(n)], 1)
                elif kind == "z":
                    act.wait_ge(projected, n + 1)
                    nc.scalar.activation(zf[:, n - NZ0, :], src, ACT.Tanh, scale=0.5).then_inc(z_tanh, 1)
                elif kind in ("ra", "rb"):
                    act.wait_ge(projected, n + 1)
                    b = kind == "rb"
                    c = 2 * ((n - NR0) // 6) + j
                    if n < NR0 + 6:
                        act.wait_ge(turned, _t)
                    else:
                        act.wait_ge(merged, 2 * ((n - NR0) // 6))
                    nc.scalar.activation(gate[:, 2 * b + j, :], src, ACT.Tanh, scale=0.5,
                                         bias=hbias[:, 8 * b + c:8 * b + c + 1]).then_inc(proj_taken[pbank(n)], 1)

            def take_turns(h):
                for f in range(h.tfills):
                    if (h.t0 + f) % 2 == 0:
                        act.wait_ge(turned, h.t0 + f + 1)
                        if h.n >= 2:
                            act.wait_ge(valued, h.n - 1)
                        n = P * len(h.blocks[4 * f:4 * f + 4])
                        nc.scalar.copy(probsT[:, h.n % 2, 512 * f:512 * f + n],
                                       ps[:, TB, 0:n]).then_inc(turn_taken[0], 1)

            def exps(h):
                for i, (at, n) in enumerate(h.rows):
                    k = [a <= i < a + c for a, c, _ in h.minima].index(True)
                    act.wait_ge(min_ready, h.m0 + k + 1)
                    row = probs[:, h.n % 2, at:at + n]
                    nc.scalar.activation(row, row, ACT.Exp, bias=nmin(h, i), scale=-1.0,
                                         accum_out=psum_den(h, i)).then_inc(exp_ready, 1)

            def by_position(g):
                if DIL[g] == 1:
                    return [(stats_dram.rearrange("(n p) c -> p n c", p=P), slice(0, P))]
                if DIL[g] == 4:
                    return [(stats_dram.rearrange("(p n) c -> p n c", p=P), slice(0, P))]
                v = stats_dram.rearrange("(i n r) c -> r i n c", n=4, r=4)
                return [(v[r], slice(32 * r, 32 * r + 32)) for r in range(4)]

            n_out = [0]

            def store_stats(g):
                act.wait_ge(exp_ready, TT * HU * (g + 1))
                for view, part in by_position(g):
                    act.dma_start(view[:, :, 8 * g:8 * g + 8], stats[part, :, 8 * g:8 * g + 8]).then_inc(stats_out, 16)
                    n_out[0] += 1

            def load_stats():
                act.wait_ge(stats_out, 16 * n_out[0])
                for g in range(NDIL):
                    for view, part in by_position(g):
                        dst = stats3[part, TT * g:TT * g + TT, :, :].rearrange("p n g c -> p n (g c)")
                        act.dma_start(dst, view).then_inc(stats_in, 16)

            for s in range(NS):
                if s + 2 < NS:
                    highs(s + 2)
                if s == 2 * OUT_AT - 3:
                    for k in range(4):
                        wo_highs(k)
                if s >= NS - 2:
                    for k in (4, 5) if s == NS - 2 else (6, 7):
                        wo_highs(k)
                take_step(s)
                if s - 1 >= 0:
                    for n in gated_in(s - 1):
                        w, c = GATED[n]
                        if w == "a":
                            act.wait_ge(dil_gated, c + 1)
                        else:
                            act.wait_ge(misc_taken, [m[1:] for m in MISC].index(("b", c)) + 1)
                        t = c if w == "a" else 2 + c
                        nc.scalar.copy(gat_hi[:, t, :], zf[:, t, :]).then_inc(gated_hi, 1)
                if s in TURNS:
                    take_turns(HEADS[TURNS[s]])
                for g in range(NDIL):
                    if s == scores_slot(HU * g + 3) + 1:
                        store_stats(g)
                if s == COEF - 1:
                    load_stats()
                if s == COEF:
                    act.wait_ge(gdif_ready, 1)
                    nc.scalar.activation(gexp[:], gdif[:], ACT.Exp).then_inc(gexp_ready, 1)
                if s in SCORES:
                    exps(HEADS[SCORES[s]])
                if s >= NR0 and step_kind(s) == "y":
                    d = ysteps(s)
                    act.wait_ge(merged, d + 1)
                    nc.scalar.copy(mrg_hi[:, d, :], ysum[:, d % 2, :]).then_inc(mrg_hi_ready, 1)

            for i in range(TT):
                for e in range(2):
                    act.wait_ge(res_added, 2 * i + e + 1)
                    nc.scalar.activation(ps[:, OUT_BANKS[2 * i + e], :], res[:, i % 2, 512 * e:512 * e + 512],
                                         ACT.Square, accum_out=ss[:, 4 + 2 * i + e:5 + 2 * i + e]).then_inc(res_squared, 1)
                act.wait_ge(out_var, i + 1)
                nc.scalar.activation(rstd[:, 4 + i:5 + i], rvar[:, 4 + i:5 + i], ACT.Sqrt).then_inc(out_rstd, 1)

        @block.vector
        def _(dve):
            chain = [0]

            def link(ins):
                ins.then_inc(dve_chain, 1)
                chain[0] += 1
                dve.wait_ge(dve_chain, chain[0])

            dve.wait_ge(vecs_turned, 1)
            link(nc.vector.tensor_copy(gb[:], ps[:, 7, 0:24]))
            nc.vector.tensor_scalar(hbias[:], gb[:, 8:24], 0.5, None, ALU.mult).then_inc(gb_ready, 1)

            def scale_rows(i):
                dve.wait_ge(rstd_ready, i + 1)
                nc.vector.tensor_scalar(xs[:, i, :], xs[:, i, :], rstd[:, i:i + 1], None,
                                        ALU.mult).then_inc(x_scaled, 1)

            for i in range(TT):
                dve.wait_ge(squared, i + 1)
                link(nc.vector.tensor_scalar(var[:, i:i + 1], ss[:, i:i + 1], 1.0 / D, EPS, ALU.mult, ALU.add))
                nc.vector.reciprocal(rvar[:, i:i + 1], var[:, i:i + 1]).then_inc(var_ready, 1)
                if i:
                    scale_rows(i - 1)
            scale_rows(TT - 1)
            for k in range(KT_D):
                dve.wait_ge(hT_hi_ready, k + 1)
                nc.vector.scalar_tensor_tensor(out=hT_lo[:, k, :], in0=ps[:, k, :], scalar=gb[:, k:k + 1],
                                               in1=hT_hi[:, k, :].bitcast(F32), op0=ALU.mult,
                                               op1=ALU.subtract).then_inc(hT_lo_ready, 1)

            def wo_lows(k):
                dve.wait_ge(wo_hi_ready, k + 1)
                nc.vector.tensor_tensor(wo("lo", k), raw_out(k), wo("hi", k).bitcast(F32),
                                        ALU.subtract).then_inc(wo_lo_ready, 1)

            def take_step(n):
                kind, u, j = step_kind(n), n // 6, n % 2
                if kind == "k":
                    dve.wait_ge(projected, n + 1)
                    if u >= 2:
                        dve.wait_ge(scored, HEADS[HU * (u - 1)].s0)
                    nc.vector.tensor_copy(residue_major(UNITS[u], KTs[:, u % 2, j, :]),
                                          residue_order(UNITS[u], ps[:, pbank(n), :])).then_inc(proj_taken[pbank(n)], 1)
                elif kind == "z":
                    z = zf[:, n - NZ0, :]
                    dve.wait_ge(z_tanh, n - NZ0 + 1)
                    nc.vector.scalar_tensor_tensor(out=z, in0=z, scalar=1.0, in1=ps[:, pbank(n), :],
                                                   op0=ALU.add, op1=ALU.mult).then_inc(proj_taken[pbank(n)], 1)

            def take_misc(m, what, at):
                dve.wait_ge(misc_ready, m + 1)
                src = ps[:, MB, :]
                if what == "v":
                    u, j = at
                    if u >= 2:
                        dve.wait_ge(valued, HU * (u - 1))
                    nc.vector.tensor_copy(Vs[:, u % 2, :, P * j:P * j + P],
                                          src.rearrange("p (t c) -> p t c", t=TT)).then_inc(misc_taken, 1)
                elif what == "a":
                    c, g = at
                    acc = dil_T[:, c, :]
                    if g == 0:
                        nc.vector.tensor_copy(acc, src).then_inc(misc_taken, 1)
                    else:
                        dve.wait_ge(misc_taken, m)
                        acc = residue_order(g, acc)
                        nc.vector.tensor_tensor(acc, residue_major(g, src), acc, ALU.add).then_inc(misc_taken, 1)
                else:
                    z = zf[:, 2 + at, :]
                    proj_taken_wait(dve, NZ0 + 2 + at)
                    nc.vector.tensor_tensor(z, src, z, ALU.mult).then_inc(misc_taken, 1)

            def gate_dilated(c):
                n = GATED.index(("a", c))
                m = [w == "a" and at == (c, NDIL - 1) for _, w, at in MISC].index(True)
                dve.wait_ge(misc_taken, m + 1)
                proj_taken_wait(dve, NZ0 + c)
                nc.vector.tensor_tensor(zf[:, c, :], dil_T[:, c, :], zf[:, c, :], ALU.mult).then_inc(dil_gated, 1)

            def gated_lows(n):
                w, c = GATED[n]
                t = c if w == "a" else 2 + c
                dve.wait_ge(gated_hi, n + 1)
                nc.vector.tensor_tensor(gat_lo[:, t, :], zf[:, t, :], gat_hi[:, t, :].bitcast(F32),
                                        ALU.subtract).then_inc(gated_lo, 1)

            def take_turns(h):
                for f in range(h.tfills):
                    if (h.t0 + f) % 2 == 1:
                        dve.wait_ge(turned, h.t0 + f + 1)
                        if h.n >= 2:
                            dve.wait_ge(valued, h.n - 1)
                        n = P * len(h.blocks[4 * f:4 * f + 4])
                        nc.vector.tensor_copy(probsT[:, h.n % 2, 512 * f:512 * f + n],
                                              ps[:, TB + 1, 0:n]).then_inc(turn_taken[1], 1)

            def mask_fill(h, f):
                lo, hi, _ = h.fills[f]
                dve.wait_ge(scored, h.s0 + f + 1)
                if h.n >= 2 and f == 0:
                    last = HEADS[h.n - 2]
                    dve.wait_ge(turned, last.t0 + last.tfills)
                src = ps[:, SB + (h.s0 + f) % 2, lo:hi]
                at = pfill(h.kind, f)
                dst = probs[:, h.n % 2, at + lo:at + hi]
                if h.kind == FULL:
                    dist = d_full[:, 512 - hi:512]
                elif h.kind == BAND:
                    dist = d_band[:, lo:hi]
                else:
                    dist = (d_quad if h.kind == QUAD else d_hex)[:, :].unsqueeze(1).broadcast_to([P, TT, P])
                    dst, src = (t.rearrange("p (i c) -> p i c", i=TT) for t in (dst, src))
                nc.vector.scalar_tensor_tensor(out=dst, in0=dist, scalar=SLOPE[h.n], in1=src, op0=ALU.mult,
                                               op1=ALU.subtract).then_inc(masked, 1)

            def min_rows(h, k):
                i, n, f = h.minima[k]
                dve.wait_ge(masked, h.s0 + f + 1)
                at, w = h.rows[i]
                src = probs[:, h.n % 2, at:at + n * w].rearrange("p (i c) -> p i c", i=n)
                nc.vector.tensor_reduce(nmin(h, i, n), src, AX.X, ALU.min).then_inc(min_ready, 1)

            def softmax_in(h):
                k = 0
                for f in range(len(h.fills)):
                    mask_fill(h, f)
                    while k < len(h.minima) and h.minima[k][2] < f:
                        min_rows(h, k)
                        k += 1
                while k < len(h.minima):
                    min_rows(h, k)
                    k += 1

            def take_values(h):
                dve.wait_ge(valued, h.n + 1)
                src = ps[:, PVB, 0:UW].rearrange("p (t c) -> p t c", t=TT)
                if h.unit < NDIL:
                    dst = o_dil[:, h.unit, :, HD * h.local:HD * h.local + HD]
                    nc.vector.tensor_copy(dst, src).then_inc(values_taken, 1)
                else:
                    n = h.n - NDIL * HU
                    dve.wait_ge(exp_ready, TT * (h.n + 1))
                    link(nc.vector.reciprocal(frec[:, n, :], fsum[:, n, :]))
                    nc.vector.tensor_tensor(o_full[:, :, HD * n:HD * n + HD], src,
                                            frec[:, n, :].unsqueeze(2).broadcast_to([P, TT, HD]),
                                            ALU.mult).then_inc(values_taken, 1)

            def coef_begin():
                dve.wait_ge(stats_in, 16 * 6)
                m = [stats3[:, :, g, 0:HU] for g in range(NDIL)]
                link(nc.vector.tensor_tensor(gmin[:], m[0], m[1], ALU.min))
                link(nc.vector.tensor_tensor(gmin[:], gmin[:], m[2], ALU.min))
                nc.vector.tensor_tensor(gdif[:], gmin[:].unsqueeze(2).broadcast_to([P, NDIL * TT, NDIL, HU]),
                                        stats3[:, :, :, 0:HU], ALU.subtract).then_inc(gdif_ready, 1)

            def coef_end():
                dve.wait_ge(gexp_ready, 1)
                link(nc.vector.tensor_tensor(gsum[:], gexp[:], stats3[:, :, :, HU:2 * HU], ALU.mult))
                link(nc.vector.tensor_tensor(gtot[:], gsum[:, :, 0, :], gsum[:, :, 1, :], ALU.add))
                link(nc.vector.tensor_tensor(gtot[:], gtot[:], gsum[:, :, 2, :], ALU.add))
                link(nc.vector.reciprocal(grec[:], gtot[:]))
                for g in range(NDIL):
                    r = slice(TT * g, TT * g + TT)
                    last = nc.vector.tensor_tensor(coef[:, r, :], gexp[:, r, g, :], grec[:, r, :], ALU.mult)
                    link(last)

            def scale_group(g):
                dve.wait_ge(values_taken, HU * (g + 1))
                o = o_dil[:, g, :, :].rearrange("p t (h c) -> p (t h) c", c=HD)
                c = coef[:, TT * g:TT * g + TT, :].rearrange("p t h -> p (t h)")
                nc.vector.tensor_tensor(o, o, c.unsqueeze(2).broadcast_to([P, TT * HU, HD]),
                                        ALU.mult).then_inc(o_scaled, 1)

            def merge(n):
                d, j = ysteps(n), n % 2
                dve.wait_ge(projected, n + 1)
                proj_taken_wait(dve, n - 2)
                proj_taken_wait(dve, n - 4)
                if d >= 1:
                    dve.wait_ge(mrg_hi_ready, d)
                link(nc.vector.scalar_tensor_tensor(out=ysum[:, 0, :] if d % 2 == 0 else ysum[:, 1, :],
                                                    in0=gate[:, j, :], scalar=1.0, in1=ps[:, SB, :],
                                                    op0=ALU.add, op1=ALU.mult))
                g = gate[:, 2 + j, :]
                nc.vector.scalar_tensor_tensor(out=g, in0=g, scalar=1.0, in1=ps[:, SB + 1, :], op0=ALU.add,
                                               op1=ALU.mult).then_inc(y_taken, 1)
                dve.wait_ge(y_taken, d + 1)
                acc = ysum[:, d % 2, :]
                nc.vector.tensor_tensor(acc, acc, g, ALU.add).then_inc(merged, 1)
                dve.wait_ge(mrg_hi_ready, d + 1)
                nc.vector.tensor_tensor(mrg_lo[:, d, :], acc, mrg_hi[:, d, :].bitcast(F32),
                                        ALU.subtract).then_inc(mrg_lo_ready, 1)

            dve.wait_ge(consts_ready, 2)
            for s in range(NS):
                if s == 2 * OUT_AT - 3:
                    for k in range(4):
                        wo_lows(k)
                if s >= NS - 2:
                    for k in (4, 5) if s == NS - 2 else (6, 7):
                        wo_lows(k)
                take_step(s)
                if s == COEF + 1:
                    coef_end()
                if COEF < s <= COEF + NDIL:
                    scale_group(s - COEF - 1)
                if s == COEF:
                    coef_begin()
                for m, (slot, what, at) in enumerate(MISC):
                    if slot == s:
                        take_misc(m, what, at)
                if s in TURNS:
                    take_turns(HEADS[TURNS[s]])
                if s in SCORES:
                    softmax_in(HEADS[SCORES[s]])
                if s in VALUES:
                    take_values(HEADS[VALUES[s]])
                if s in GATED_A:
                    gate_dilated(GATED_A[s])
                for n in gated_in(s - 1):
                    gated_lows(n)
                if step_kind(s) == "y":
                    merge(s)

            dve.wait_ge(fg_in, 16)
            for i in range(TT):
                dve.wait_ge(res_in[i % 2], 16 * (i // 2 + 1))
                r = res[:, i % 2, :]
                for e in range(2):
                    half = r[:, 512 * e:512 * e + 512]
                    dve.wait_ge(out_ready, 2 * i + e + 1)
                    nc.vector.scalar_tensor_tensor(out=half, in0=ps[:, OUT_BANKS[2 * i + e], :], scalar=0.25,
                                                   in1=half, op0=ALU.mult, op1=ALU.add).then_inc(res_added, 1)
                dve.wait_ge(res_squared, 2 * i + 2)
                a = 4 + 2 * i
                link(nc.vector.tensor_tensor(var[:, 4 + i:5 + i], ss[:, a:a + 1], ss[:, a + 1:a + 2], ALU.add))
                link(nc.vector.tensor_scalar(var[:, 4 + i:5 + i], var[:, 4 + i:5 + i], 1.0 / D, EPS,
                                             ALU.mult, ALU.add))
                nc.vector.reciprocal(rvar[:, 4 + i:5 + i], var[:, 4 + i:5 + i]).then_inc(out_var, 1)
                dve.wait_ge(out_rstd, i + 1)
                nc.vector.scalar_tensor_tensor(out=r, in0=r, scalar=rstd[:, 4 + i:5 + i], in1=fg[:], op0=ALU.mult,
                                               op1=ALU.mult).then_inc(out_done, 1)


_INS = ["x", "norm_g", "w_in", "b_merge", "w_pa", "w_pb", "w_out", "final_g"]
_FLAT = {"w_in", "w_pa", "w_pb", "w_out"}


def kernel(**inputs):
    import concourse.bacc as bacc
    from concourse.bass_utils import run_bass_kernel_spmd

    nc = bacc.Bacc("TRN2", target_bir_lowering=False, num_devices=1)
    arrays, args = {}, []
    for name in _INS:
        a = np.ascontiguousarray(inputs[name])
        if name in _FLAT:
            a = a.reshape(a.shape[1:])
        arrays[f"in_{name}"] = a
        args.append(nc.dram_tensor(f"in_{name}", a.shape, mybir.dt.from_np(a.dtype), kind="ExternalInput").ap())
    out = nc.dram_tensor("out_0", (1, SEQ, D), F32, kind="ExternalOutput").ap()
    hybrid_layer_program(nc, *args, out)
    r = run_bass_kernel_spmd(nc, [arrays], core_ids=[0])
    return r.results[0]["out_0"]
```

```python
from contextlib import ExitStack

import concourse.bass as bass
from concourse import mybir
import numpy as np

F32 = mybir.dt.float32
F32R = mybir.dt.float32r
I32 = mybir.dt.int32
ALU = mybir.AluOpType
ACT = mybir.ActivationFunctionType
AX = mybir.AxisListType

P = 128
SEQ = 512
D = 1024
TT = SEQ // P
KT_D = D // P
HD = 64
HU = 4
UW = HU * HD
EPS = 1e-6
BIG = 1e32

BAND, QUAD, HEX, FULL = range(4)
UNITS = [BAND, QUAD, HEX, FULL, FULL]
NU = len(UNITS)
NH = NU * HU
NDIL = 3
DIL = [1, 4, 16]
C_A = NDIL * 3 * UW
C_ZA = C_A
C_B = C_ZA + UW
C_ZB = C_B + 3 * 2 * UW
C_RA = C_ZB + 2 * UW
C_RB = C_RA + D


def slopes(n):
    return [float(np.float32(2.0 ** (-8.0 * (i + 1) / n))) for i in range(n)]


SLOPE = slopes(NDIL * HU) + slopes(2 * HU)

CHUNKS = []
for u, kind in enumerate(UNITS):
    q = u * 3 * UW if u < NDIL else C_B + (u - NDIL) * UW
    w = UW if u < NDIL else 2 * UW
    CHUNKS += [("k", q + w), ("q", q), ("v", q + 2 * w)]
CHUNKS += [("z", C_ZA), ("z", C_ZB), ("z", C_ZB + UW)]
NZ0 = 2 * 3 * NU
NR0 = NZ0 + 6
ND = D // P
for j in range(ND // 2):
    CHUNKS += [("ra", C_RA + 256 * j), ("rb", C_RB + 256 * j), ("y", 256 * j)]
NS = 2 * len(CHUNKS)
OUT_AT = len(CHUNKS) - 3
LOADS = [("w", c) for c in range(OUT_AT)] + [("out", 0), ("out", 1)] + \
        [("w", c) for c in range(OUT_AT, len(CHUNKS))] + [("out", 2), ("out", 3)]
NRAW = 3
WARM = 14
NRING = 4
LOAD_OF = {item: n for n, item in enumerate(LOADS)}


def step_kind(n):
    return CHUNKS[n // 2][0]


def pbank(n):
    return n % 2


def puse(n):
    return sum(1 for m in range(n) if m % 2 == n % 2 and step_kind(m) != "y")


def ysteps(n):
    return sum(1 for m in range(n) if step_kind(m) == "y")


def fills(kind):
    if kind == FULL:
        return [(0, P * (i + 1), [(i, 0, 0, P * (i + 1))]) for i in range(TT)]
    if kind == BAND:
        return [(P, 512, [(0, P, 0, P), (1, 256, 0, 256)]),
                (0, 512, [(2, 0, P, 256), (3, 256, 2 * P, 256)])]
    return [(0, 512, [(i, P * i, P * i, P) for i in range(TT)])]


def prow(kind):
    if kind == FULL:
        return [(P * i * (i + 1) // 2, P * (i + 1)) for i in range(TT)]
    if kind == BAND:
        return [(P, P), (256, 256), (512, 256), (768, 256)]
    return [(P * i, P) for i in range(TT)]


def pfill(kind, f):
    if kind == FULL:
        return P * f * (f + 1) // 2
    return 512 * f


def blocks(kind):
    out = []
    for i, (at, n) in enumerate(prow(kind)):
        for b in range(n // P):
            kt = b if kind == FULL else (i - n // P + 1 + b if kind == BAND else i)
            out.append((i, kt, at + P * b))
    return out


def minima(kind):
    if kind == FULL:
        return [(i, 1, i) for i in range(TT)]
    if kind == BAND:
        return [(0, 1, 0), (1, 1, 0), (2, 2, 1)]
    return [(0, TT, 0)]


class Head:
    pass


HEADS = []
_s = _m = _t = 0
for h in range(NH):
    x = Head()
    x.n, x.unit, x.kind = h, h // HU, UNITS[h // HU]
    x.local, x.pair, x.part = h % HU, (h % HU) // 2, HD * (h % 2)
    x.fills, x.rows, x.blocks, x.minima = fills(x.kind), prow(x.kind), blocks(x.kind), minima(x.kind)
    x.s0, x.m0, x.t0 = _s, _m, _t
    x.tfills = -(-len(x.blocks) // 4)
    _s, _m, _t = _s + len(x.fills), _m + len(x.minima), _t + x.tfills
    HEADS.append(x)


def scores_slot(h):
    return 6 * (h // HU + 1) + h % HU


SCORES = {scores_slot(h): h for h in range(NH)}
TURNS = {scores_slot(h) + 1: h for h in range(NH)}
VALUES = {scores_slot(h) + 2: h for h in range(NH)}

MISC = []
COEF = scores_slot(NDIL * HU - 1) + 3
MISC += [(COEF + 2 + 3 * c + g, "a", (c, g)) for c in range(2) for g in range(NDIL)]
MISC += [(NZ0 + 3 + c, "b", c) for c in range(4)]
MISC.sort(key=lambda m: m[0])
GATED_A = {NZ0 + 2: 0, NZ0 + 3: 1}
GATED_B = {NZ0 + 3 + c: c for c in range(4)}
GATED = [("a", 0), ("a", 1), ("b", 0), ("b", 1), ("b", 2), ("b", 3)]
assert COEF + 7 < NZ0 + 2


def gated_in(slot):
    return [n for n, (w, c) in enumerate(GATED)
            if (GATED_A if w == "a" else GATED_B).get(slot) == c]


def hybrid_layer_program(nc, x, norm_g, w_in, b_merge, w_pa, w_pb, w_out, final_g, out):
    stats_dram = nc.dram_tensor("stats_by_position", (SEQ, NDIL * 8), F32, kind="Internal").ap()
    top = ExitStack()
    with top:
        def sb(name, shape, dt, stack=top):
            return stack.enter_context(nc.sbuf_tensor(name, shape, dt))

        def sem(name):
            return top.enter_context(nc.semaphore(name))

        raw = sb("raw", [P, NRAW, 2048], F32)
        w_hi = sb("w_hi", [P, NRING, 1024], F32R)
        w_lo = sb("w_lo", [P, NRING, 1024], F32R)
        gat_hi = sb("gat_hi", [P, 6, SEQ], F32R)
        gat_lo = sb("gat_lo", [P, 6, SEQ], F32R)
        fg = sb("fg", [P, D], F32)
        d_full = sb("d_full", [P, 512], F32)
        d_band = sb("d_band", [P, 512], F32)
        d_quad = sb("d_quad", [P, P], F32)
        d_hex = sb("d_hex", [P, P], F32)
        ident = sb("ident", [P, P], F32)
        vecs = sb("vecs", [24, P], F32)
        gb = sb("gb", [P, 24], F32)
        hbias = sb("hbias", [P, 16], F32)
        ss = sb("ss", [P, 16], F32)
        unread = sb("unread", [P, 1], F32)
        var = sb("var", [P, 8], F32)
        rvar = sb("rvar", [P, 8], F32)
        rstd = sb("rstd", [P, 8], F32)

        hstack = ExitStack()
        hT_hi = sb("hT_hi", [P, KT_D, SEQ], F32R, hstack)
        hT_lo = sb("hT_lo", [P, KT_D, SEQ], F32R, hstack)
        xstack = ExitStack()
        xs = sb("xs", [P, TT, D], F32, xstack)
        squares = sb("squares", [P, TT, D], F32, xstack)
        xstack.close()
        astack = ExitStack()
        probs = sb("probs", [P, 2, 1280], F32, astack)
        KTs = sb("KTs", [P, 2, 2, SEQ], F32, astack)
        QTs = sb("QTs", [P, 2, 2, SEQ], F32, astack)
        Vs = sb("Vs", [P, 2, TT, UW], F32, astack)
        probsT = sb("probsT", [P, 2, 1280], F32, astack)
        o_dil = sb("o_dil", [P, NDIL, TT, UW], F32, astack)
        o_full = sb("o_full", [P, TT, 2 * UW], F32, astack)
        zf = sb("zf", [P, 6, SEQ], F32, astack)
        dil_T = sb("dil_T", [P, 2, SEQ], F32, astack)
        stats = sb("stats", [P, TT, NDIL * 8], F32, astack)
        stats3 = sb("stats3", [P, NDIL * TT, NDIL, 8], F32, astack)
        gmin = sb("gmin", [P, NDIL * TT, HU], F32, astack)
        gdif = sb("gdif", [P, NDIL * TT, NDIL, HU], F32, astack)
        gexp = sb("gexp", [P, NDIL * TT, NDIL, HU], F32, astack)
        gsum = sb("gsum", [P, NDIL * TT, NDIL, HU], F32, astack)
        gtot = sb("gtot", [P, NDIL * TT, HU], F32, astack)
        grec = sb("grec", [P, NDIL * TT, HU], F32, astack)
        coef = sb("coef", [P, NDIL * TT, HU], F32, astack)
        fmin = sb("fmin", [P, 2 * HU, TT], F32, astack)
        fsum = sb("fsum", [P, 2 * HU, TT], F32, astack)
        frec = sb("frec", [P, 2 * HU, TT], F32, astack)
        astack.close()
        hstack.close()
        wo_b_hi = sb("wo_b_hi", [P, 3, D], F32R)
        wo_b_lo = sb("wo_b_lo", [P, 3, D], F32R)
        res = sb("res", [P, 2, D], F32)
        gate = sb("gate", [P, 4, SEQ], F32)
        wo_a_hi = sb("wo_a_hi", [P, 5, D], F32R)
        wo_a_lo = sb("wo_a_lo", [P, 5, D], F32R)
        mrg_hi = sb("mrg_hi", [P, ND, SEQ], F32R)
        mrg_lo = sb("mrg_lo", [P, ND, SEQ], F32R)
        ysum = sb("ysum", [P, 2, SEQ], F32)

        ps = top.enter_context(nc.psum_tensor("ps", [P, 8, 512], F32))
        def ybank(n):
            return SB if ysteps(n) % 2 == 0 else TB

        SB, TB, PVB, MB = 2, 4, 6, 7
        OUT_BANKS = [6, 7, 0, 1, 2, 3, 4, 5]

        x_in = [sem(f"x_in{i}") for i in range(TT)]
        vec_in = sem("vec_in")
        fg_in = sem("fg_in")
        raw_in = [sem(f"raw_in{i}") for i in range(NRAW)]
        const_step = sem("const_step")
        consts_ready = sem("consts_ready")
        squared = sem("squared")
        act_chain = sem("act_chain")
        dve_chain = sem("dve_chain")
        var_ready = sem("var_ready")
        rstd_ready = sem("rstd_ready")
        x_scaled = sem("x_scaled")
        vecs_turned = sem("vecs_turned")
        gb_ready = sem("gb_ready")
        x_turned = sem("x_turned")
        hT_hi_ready = sem("hT_hi_ready")
        hT_lo_ready = sem("hT_lo_ready")
        hi_ready = sem("hi_ready")
        lo_ready = sem("lo_ready")
        wo_hi_ready = sem("wo_hi_ready")
        wo_lo_ready = sem("wo_lo_ready")
        projected = sem("projected")
        proj_taken = [sem(f"proj_taken{b}") for b in range(2)]
        z_tanh = sem("z_tanh")
        misc_ready = sem("misc_ready")
        misc_taken = sem("misc_taken")
        scored = sem("scored")
        masked = sem("masked")
        min_ready = sem("min_ready")
        exp_ready = sem("exp_ready")
        turned = sem("turned")
        turn_taken = [sem(f"turn_taken{b}") for b in range(2)]
        valued = sem("valued")
        values_taken = sem("values_taken")
        stats_out = sem("stats_out")
        stats_in = sem("stats_in")
        gdif_ready = sem("gdif_ready")
        gexp_ready = sem("gexp_ready")
        o_scaled = sem("o_scaled")
        dil_gated = sem("dil_gated")
        gated_hi = sem("gated_hi")
        gated_lo = sem("gated_lo")
        y_taken = sem("y_taken")
        merged = sem("merged")
        mrg_hi_ready = sem("mrg_hi_ready")
        mrg_lo_ready = sem("mrg_lo_ready")
        out_ready = sem("out_ready")
        res_in = [sem(f"res_in{i}") for i in range(2)]
        res_added = sem("res_added")
        res_squared = sem("res_squared")
        out_var = sem("out_var")
        out_rstd = sem("out_rstd")
        out_done = sem("out_done")
        stored = [sem(f"stored{i}") for i in range(2)]

        w_in_t = w_in.rearrange("(k p) c -> p k c", p=P)
        w_pa_t = w_pa.rearrange("(k p) c -> p k c", p=P)
        w_pb_t = w_pb.rearrange("(k p) c -> p k c", p=P)
        w_out_t = w_out.rearrange("(k p) c -> p k c", p=P)
        x_t = x.rearrange("b (n p) d -> p (b n) d", p=P)
        out_t = out.rearrange("b (n p) d -> p (b n) d", p=P)

        def raw_waits(item):
            n = LOAD_OF[item]
            count = 0
            for m in range(n % NRAW, n + 1, NRAW):
                k, c = LOADS[m]
                count += 32 if k == "w" and CHUNKS[c][0] == "y" else 16
            return raw_in[n % NRAW], count

        def halves_before(n):
            return (2 * sum(1 for k, _ in LOADS[:n + 1] if k == "w"),
                    2 * sum(1 for k, _ in LOADS[:n + 1] if k == "out"))

        def raw_half(n):
            slot = LOAD_OF[("w", n // 2)] % NRAW
            kt = 6 if step_kind(n) == "y" else KT_D
            return raw[:, slot, 0:kt * 256].rearrange("p (k c) -> p k c", k=kt)[:, :, P * (n % 2):P * (n % 2) + P], kt

        def ring(t, n, kt):
            return t[:, n % NRING, 0:kt * P].rearrange("p (k c) -> p k c", k=kt)

        def raw_out(k):
            return raw[:, LOAD_OF[("out", k // 2)] % NRAW, D * (k % 2):D * (k % 2) + D]

        def wo(part, k):
            a, b = (wo_a_hi, wo_b_hi) if part == "hi" else (wo_a_lo, wo_b_lo)
            return a[:, k, :] if k < 5 else b[:, k - 5, :]

        def pair_ring(t, n):
            at = n // 2 * 2 % NRING
            return t[:, at:at + 2, :]

        def rows_of(kind, t, i):
            if kind in (QUAD, HEX):
                return t.rearrange("p (i r) -> p r i", r=TT)[:, i, :]
            return t[:, P * i:P * i + P]

        def residue_order(kind, t):
            return t if kind in (BAND, FULL) else t.rearrange("p (i r) -> p r i", r=TT)

        def residue_major(kind, t):
            return t if kind in (BAND, FULL) else t.rearrange("p (r i) -> p r i", r=TT)

        def nmin(h, i, n=1):
            if h.unit < NDIL:
                return stats[:, i:i + n, 8 * h.unit + h.local]
            return fmin[:, h.n - NDIL * HU, i:i + n]

        def psum_den(h, i):
            if h.unit < NDIL:
                return stats[:, i, 8 * h.unit + HU + h.local:8 * h.unit + HU + h.local + 1]
            return fsum[:, h.n - NDIL * HU, i:i + 1]

        def turn_taken_wait(eng, fill):
            eng.wait_ge(turn_taken[fill % 2], fill // 2 + 1)

        def proj_taken_wait(eng, n):
            eng.wait_ge(proj_taken[pbank(n)], puse(n) + 1)

        block = top.enter_context(nc.Block())

        @block.sync
        def _(sp):
            for i in range(TT):
                sp.dma_start(xs[:, i, :], x_t[:, i, :]).then_inc(x_in[i], 16)
            for n, (k, c) in enumerate(LOADS):
                if n >= NRAW:
                    ring_n, out_n = halves_before(n - NRAW)
                    sp.wait_ge(hi_ready, ring_n)
                    sp.wait_ge(lo_ready, ring_n)
                    if out_n:
                        sp.wait_ge(wo_hi_ready, out_n)
                        sp.wait_ge(wo_lo_ready, out_n)
                slot, s = raw[:, n % NRAW, :], raw_in[n % NRAW]
                if k == "out":
                    sp.dma_start(slot.rearrange("p (k c) -> p k c", k=2), w_out_t[:, 2 * c:2 * c + 2, :]).then_inc(s, 16)
                elif CHUNKS[c][0] == "y":
                    at = CHUNKS[c][1]
                    dst = slot[:, 0:6 * 256].rearrange("p (k c) -> p k c", k=6)
                    sp.dma_start(dst[:, 0:2, :], w_pa_t[:, :, at:at + 256]).then_inc(s, 16)
                    sp.dma_start(dst[:, 2:6, :], w_pb_t[:, :, at:at + 256]).then_inc(s, 16)
                else:
                    at = CHUNKS[c][1]
                    sp.dma_start(slot.rearrange("p (k c) -> p k c", k=KT_D), w_in_t[:, :, at:at + 256]).then_inc(s, 16)
                if n == 3:
                    sp.dma_start(fg[:, :], final_g.partition_broadcast(P)).then_inc(fg_in, 16)
            sp.wait_ge(projected, NS - 2)
            for i in range(2):
                sp.dma_start(res[:, i, :], x_t[:, i, :]).then_inc(res_in[i], 16)
            for i in range(TT):
                sp.wait_ge(out_done, i + 1)
                sp.dma_start(out_t[:, i, :], res[:, i % 2, :]).then_inc(stored[i % 2], 16)
                if i + 2 < TT:
                    sp.wait_ge(stored[i % 2], 16)
                    sp.dma_start(res[:, i % 2, :], x_t[:, i + 2, :]).then_inc(res_in[i % 2], 16)
            for i in range(2):
                sp.wait_ge(stored[i], 32)

        @block.gpsimd
        def _(pool):
            steps = [0]

            def link(ins):
                ins.then_inc(const_step, 1)
                steps[0] += 1
                pool.wait_ge(const_step, steps[0])

            link(nc.gpsimd.memset(ident[:], 0.0))
            nc.gpsimd.affine_select(out=ident[:], in_=ident[:], compare_op=ALU.not_equal, fill=1.0, base=0,
                                    pattern=[[-1, P]], channel_multiplier=1).then_inc(consts_ready, 1)
            pool.wait_ge(consts_ready, 1)

            def lows(n):
                pool.wait_ge(hi_ready, n + 1)
                s, count = raw_waits(("w", n // 2))
                pool.wait_ge(s, count)
                if n >= NRING:
                    pool.wait_ge(projected, n - 2)
                src, kt = raw_half(n)
                nc.gpsimd.tensor_tensor(ring(w_lo, n, kt), src, ring(w_hi, n, kt).bitcast(F32),
                                        ALU.subtract).then_inc(lo_ready, 1)

            link(nc.gpsimd.iota(d_full[:], [[-1, 512]], base=384, channel_multiplier=1,
                                allow_small_or_imprecise_dtypes=True))
            link(nc.gpsimd.affine_select(out=d_full[:], in_=d_full[:], compare_op=ALU.is_ge, fill=BIG, base=384,
                                         pattern=[[-1, 512]], channel_multiplier=1))
            band = d_band[:].rearrange("p (a c) -> p a c", a=2)
            link(nc.gpsimd.iota(band, [[0, 2], [-1, 256]], base=P, channel_multiplier=1,
                                allow_small_or_imprecise_dtypes=True))
            link(nc.gpsimd.affine_select(out=band, in_=band, compare_op=ALU.is_ge, fill=BIG, base=P,
                                         pattern=[[0, 2], [-1, 256]], channel_multiplier=1))
            link(nc.gpsimd.affine_select(out=band, in_=band, compare_op=ALU.is_ge, fill=BIG, base=0,
                                         pattern=[[0, 2], [1, 256]], channel_multiplier=-1))
            link(nc.gpsimd.iota(d_quad[:], [[-4, P]], base=0, channel_multiplier=4,
                                allow_small_or_imprecise_dtypes=True))
            link(nc.gpsimd.affine_select(out=d_quad[:], in_=d_quad[:], compare_op=ALU.is_ge, fill=BIG, base=0,
                                         pattern=[[-1, P]], channel_multiplier=1))
            nc.gpsimd.iota(d_hex[:].bitcast(I32), [[-1, P]], base=0, channel_multiplier=1).then_inc(consts_ready, 1)
            pool.wait_ge(consts_ready, 2)
            for n in range(NS):
                lows(n)

        @block.tensor
        def _(pe):
            pe.wait_ge(consts_ready, 1)
            for _ in range(WARM):
                pe.matmul(ps[:, 0, 0:P], ident[:, :], ident[:, :], start=True, stop=True)
            pe.wait_ge(vec_in, 32)
            pe.transpose(ps[:, 7, 0:24], vecs[:, :], ident[0:24, 0:24]).then_inc(vecs_turned, 1)
            for i in range(TT):
                pe.wait_ge(x_scaled, i + 1)
                if i == 0:
                    pe.wait_ge(gb_ready, 1)
                for k in range(KT_D):
                    last = pe.transpose(ps[:, k, P * i:P * i + P], xs[:, i, P * k:P * k + P], ident[:, :])
                last.then_inc(x_turned, 1)

            def weights_wait(n):
                pe.wait_ge(hi_ready, n + 1)
                pe.wait_ge(lo_ready, n + 1)

            def term(out, k, kts, wh, wl, hh, hl):
                pe.matmul(out, wh, hh, start=(k == 0), stop=False)
                pe.matmul(out, wh, hl, start=False, stop=False)
                return pe.matmul(out, wl, hh, start=False, stop=(k == kts - 1))

            def step_pieces(n):
                kind = step_kind(n)

                def start():
                    weights_wait(n)
                    if kind == "v":
                        weights_wait(n // 2 * 2 + 1)
                    if kind == "y":
                        if ysteps(n) == 0:
                            pe.wait_ge(gated_hi, 6)
                            pe.wait_ge(gated_lo, 6)
                            pe.wait_ge(masked, _s)
                            turn_taken_wait(pe, _t - 1)
                            turn_taken_wait(pe, _t - 2)
                        if ysteps(n) >= 2:
                            pe.wait_ge(y_taken, ysteps(n) - 1)
                    elif puse(n):
                        pe.wait_ge(proj_taken[pbank(n)], puse(n))

                def column_tile(k):
                    if n < 2:
                        pe.wait_ge(hT_lo_ready, max(k, n) + 1)
                    last = term(ps[:, pbank(n), :], k, KT_D, ring(w_hi, n, KT_D)[:, k, :],
                                ring(w_lo, n, KT_D)[:, k, :], hT_hi[:, k, :], hT_lo[:, k, :])
                    if k == KT_D - 1:
                        last.then_inc(projected, 1)

                def value_rows(i, ks):
                    kind_u = UNITS[n // 6]
                    t = 2 * (n % 2) + i
                    for k in ks:
                        hh, hl = (rows_of(kind_u, h[:, k, :], t) for h in (hT_hi, hT_lo))
                        wh, wl = (pair_ring(w, n)[:, :, P * k:P * k + P] for w in (w_hi, w_lo))
                        o = ps[:, pbank(n), UW * i:UW * i + UW].rearrange("p (j c) -> p j c", j=2)
                        pe.matmul(o, hh, wh, start=(k == 0), stop=False)
                        pe.matmul(o, hl, wh, start=False, stop=False)
                        last = pe.matmul(o, hh, wl, start=False, stop=(k == KT_D - 1))
                    if i == 1 and ks[-1] == KT_D - 1:
                        last.then_inc(projected, 1)

                def branches(ks):
                    for k in ks:
                        b = k >= 2
                        last = term(ps[:, ybank(n) + b, :], k - 2 * b, 4 if b else 2, ring(w_hi, n, 6)[:, k, :],
                                    ring(w_lo, n, 6)[:, k, :], gat_hi[:, k, :], gat_lo[:, k, :])
                    if ks[-1] == 5:
                        last.then_inc(projected, 1)

                if kind == "v":
                    pieces = [lambda i=i, k=k: value_rows(i, [k, k + 1]) for i in range(2) for k in range(0, KT_D, 2)]
                elif kind == "y":
                    pieces = [lambda k=k: branches([k, k + 1]) for k in range(0, 6, 2)]
                else:
                    pieces = [lambda k=k: column_tile(k) for k in range(KT_D)]
                first = pieces[0]
                pieces[0] = lambda: (start(), first())
                return pieces

            def turn_misc(m, what, at):
                if m:
                    pe.wait_ge(misc_taken, m)
                if what == "a":
                    c, g = at
                    pe.wait_ge(o_scaled, g + 1)
                    src = [o_dil[:, g, t, P * c:P * c + P] for t in range(TT)]
                else:
                    pe.wait_ge(values_taken, NDIL * HU + 2 * at + 2)
                    src = [o_full[:, t, P * at:P * at + P] for t in range(TT)]
                for t in range(TT):
                    last = pe.transpose(ps[:, MB, P * t:P * t + P], src[t], ident[:, :])
                last.then_inc(misc_ready, 1)

            def scores(h, f):
                u = h.unit
                if f == 0:
                    proj_taken_wait(pe, 6 * u + h.pair)
                    proj_taken_wait(pe, 6 * u + 2 + h.pair)
                K, Q = (t[h.part:h.part + HD, u % 2, h.pair, :] for t in (KTs, QTs))
                for f, (_, _, tiles) in [(f, h.fills[f])]:
                    if h.s0 + f >= 2:
                        pe.wait_ge(masked, h.s0 + f - 1)
                    for i, at, k0, nk in tiles:
                        last = pe.matmul(ps[:, SB + (h.s0 + f) % 2, at:at + nk], Q[:, P * i:P * i + P],
                                         K[:, k0:k0 + nk], start=True, stop=True)
                    last.then_inc(scored, 1)

            def turns(h, f):
                for f in [f]:
                    if h.t0 + f >= 2:
                        turn_taken_wait(pe, h.t0 + f - 2)
                    for b, (i, _, at) in enumerate(h.blocks[4 * f:4 * f + 4]):
                        pe.wait_ge(exp_ready, TT * h.n + i + 1)
                        last = pe.transpose(ps[:, TB + (h.t0 + f) % 2, P * b:P * b + P],
                                            probs[:, h.n % 2, at:at + P], ident[:, :])
                    last.then_inc(turned, 1)

            def values(h):
                for f in range(h.tfills):
                    turn_taken_wait(pe, h.t0 + f)
                if h.n:
                    pe.wait_ge(values_taken, h.n)
                for j in range(2):
                    proj_taken_wait(pe, 6 * h.unit + 4 + j)
                for i in range(TT):
                    mine = [(b, kt) for b, (q, kt, _) in enumerate(h.blocks) if q == i]
                    for b, kt in mine:
                        last = pe.matmul(ps[:, PVB, HD * i:HD * i + HD], probsT[:, h.n % 2, P * b:P * b + P],
                                         Vs[:, h.unit % 2, kt, HD * h.local:HD * h.local + HD],
                                         start=((b, kt) == mine[0]), stop=((b, kt) == mine[-1]))
                last.then_inc(valued, 1)

            for s in range(NS):
                between = []
                for m, (slot, what, at) in enumerate(MISC):
                    if slot == s:
                        between.append(lambda m=m, what=what, at=at: turn_misc(m, what, at))
                if s in VALUES:
                    between.append(lambda: values(HEADS[VALUES[s]]))
                if s in TURNS:
                    h = HEADS[TURNS[s]]
                    between += [lambda h=h, f=f: turns(h, f) for f in range(h.tfills)]
                if s in SCORES:
                    h = HEADS[SCORES[s]]
                    between += [lambda h=h, f=f: scores(h, f) for f in range(len(h.fills))]
                pieces = step_pieces(s)
                n, m = len(pieces), len(between)
                for i, piece in enumerate(pieces):
                    piece()
                    for other in between[m * i // n:m * (i + 1) // n]:
                        other()

            for i in range(TT):
                banks = [OUT_BANKS[2 * i], OUT_BANKS[2 * i + 1]]
                if 2 in banks or 4 in banks:
                    pe.wait_ge(y_taken, ysteps(NS) - (4 in banks) * (ybank(NS - 1) != 4))
                if 0 in banks:
                    proj_taken_wait(pe, NS - 3)
                    proj_taken_wait(pe, NS - 4)
                if MB in banks:
                    pe.wait_ge(misc_taken, len(MISC))
                    pe.wait_ge(values_taken, NH)
                order = [(k, e) for k in range(KT_D) for e in range(2)] if i == 0 else \
                        [(k, e) for e in range(2) for k in range(KT_D)]
                for k, e in order:
                    if i == 0 and e == 0:
                        pe.wait_ge(wo_lo_ready, k + 1)
                        pe.wait_ge(wo_hi_ready, k + 1)
                        pe.wait_ge(mrg_hi_ready, k + 1)
                        pe.wait_ge(mrg_lo_ready, k + 1)
                    o, cols = ps[:, banks[e], :], slice(512 * e, 512 * e + 512)
                    mh, ml = mrg_hi[:, k, P * i:P * i + P], mrg_lo[:, k, P * i:P * i + P]
                    pe.matmul(o, mh, wo("hi", k)[:, cols], start=(k == 0), stop=False)
                    pe.matmul(o, mh, wo("lo", k)[:, cols], start=False, stop=False)
                    last = pe.matmul(o, ml, wo("hi", k)[:, cols], start=False, stop=(k == KT_D - 1))
                    if k == KT_D - 1:
                        last.then_inc(out_ready, 1)

        @block.scalar
        def _(act):
            def highs(n):
                s, count = raw_waits(("w", n // 2))
                act.wait_ge(s, count)
                if n >= NRING:
                    act.wait_ge(projected, n - 2)
                src, kt = raw_half(n)
                nc.scalar.copy(ring(w_hi, n, kt), src).then_inc(hi_ready, 1)

            def wo_highs(k):
                s, count = raw_waits(("out", k // 2))
                act.wait_ge(s, count)
                if k == 0:
                    act.wait_ge(gated_lo, 6)
                    act.wait_ge(gated_hi, 6)
                if k == 5:
                    act.wait_ge(projected, NS - 2)
                nc.scalar.copy(wo("hi", k), raw_out(k)).then_inc(wo_hi_ready, 1)

            act.dma_start(vecs[0:8, :], norm_g.rearrange("l (k p) -> (l k) p", p=P)).then_inc(vec_in, 16)
            act.dma_start(vecs[8:24, :], b_merge.rearrange("l (k p) -> (l k) p", p=P)).then_inc(vec_in, 16)
            act.wait_ge(consts_ready, 1)
            nc.scalar.activation(unread[:], ident[:, 0:1], ACT.Sqrt)
            for i in range(TT):
                act.wait_ge(x_in[i], 16)
                nc.scalar.activation(squares[:, i, :], xs[:, i, :], ACT.Square,
                                     accum_out=ss[:, i:i + 1]).then_inc(squared, 1)
                if i:
                    act.wait_ge(var_ready, i)
                    nc.scalar.activation(rstd[:, i - 1:i], rvar[:, i - 1:i], ACT.Sqrt).then_inc(rstd_ready, 1)
            act.wait_ge(var_ready, TT)
            nc.scalar.activation(rstd[:, TT - 1:TT], rvar[:, TT - 1:TT], ACT.Sqrt).then_inc(rstd_ready, 1)
            highs(0)
            highs(1)
            act.wait_ge(x_turned, TT)
            act.wait_ge(gb_ready, 1)
            for k in range(KT_D):
                nc.scalar.activation(hT_hi[:, k, :], ps[:, k, :], ACT.Copy,
                                     scale=gb[:, k:k + 1]).then_inc(hT_hi_ready, 1)

            def take_step(n):
                kind = step_kind(n)
                u, j = n // 6, n % 2
                src = ps[:, pbank(n), :]
                if kind in ("q", "v"):
                    act.wait_ge(projected, n + 1)
                    if kind == "q":
                        if u >= 2:
                            act.wait_ge(scored, HEADS[HU * (u - 1)].s0)
                        dst = QTs[:, u % 2, j, :]
                        nc.scalar.activation(residue_major(UNITS[u], dst), residue_order(UNITS[u], src), ACT.Copy,
                                             scale=HD ** -0.5).then_inc(proj_taken[pbank(n)], 1)
                    else:
                        if u >= 2:
                            act.wait_ge(valued, HU * (u - 1))
                        nc.scalar.copy(Vs[:, u % 2, 2 * j:2 * j + 2, :].rearrange("p t c -> p (t c)"),
                                       src).then_inc(proj_taken[pbank(n)], 1)
                elif kind == "z":
                    act.wait_ge(projected, n + 1)
                    nc.scalar.activation(zf[:, n - NZ0, :], src, ACT.Tanh, scale=0.5).then_inc(z_tanh, 1)
                elif kind in ("ra", "rb"):
                    act.wait_ge(projected, n + 1)
                    b = kind == "rb"
                    c = 2 * ((n - NR0) // 6) + j
                    if n < NR0 + 6:
                        act.wait_ge(turned, _t)
                    else:
                        act.wait_ge(merged, 2 * ((n - NR0) // 6))
                    nc.scalar.activation(gate[:, 2 * b + j, :], src, ACT.Tanh, scale=0.5,
                                         bias=hbias[:, 8 * b + c:8 * b + c + 1]).then_inc(proj_taken[pbank(n)], 1)

            def take_turns(h):
                for f in range(h.tfills):
                    if (h.t0 + f) % 2 == 0:
                        act.wait_ge(turned, h.t0 + f + 1)
                        if h.n >= 2:
                            act.wait_ge(valued, h.n - 1)
                        n = P * len(h.blocks[4 * f:4 * f + 4])
                        nc.scalar.copy(probsT[:, h.n % 2, 512 * f:512 * f + n],
                                       ps[:, TB, 0:n]).then_inc(turn_taken[0], 1)

            def exps(h):
                for i, (at, n) in enumerate(h.rows):
                    k = [a <= i < a + c for a, c, _ in h.minima].index(True)
                    act.wait_ge(min_ready, h.m0 + k + 1)
                    row = probs[:, h.n % 2, at:at + n]
                    nc.scalar.activation(row, row, ACT.Exp, bias=nmin(h, i), scale=-1.0,
                                         accum_out=psum_den(h, i)).then_inc(exp_ready, 1)

            def by_position(g):
                if DIL[g] == 1:
                    return [(stats_dram.rearrange("(n p) c -> p n c", p=P), slice(0, P))]
                return [(stats_dram.rearrange("(p n) c -> p n c", p=P), slice(0, P))]

            n_out = [0]

            def store_stats(g):
                act.wait_ge(exp_ready, TT * HU * (g + 1))
                for view, part in by_position(g):
                    act.dma_start(view[:, :, 8 * g:8 * g + 8], stats[part, :, 8 * g:8 * g + 8]).then_inc(stats_out, 16)
                    n_out[0] += 1

            def load_stats():
                act.wait_ge(stats_out, 16 * n_out[0])
                for g in range(NDIL):
                    for view, part in by_position(g):
                        dst = stats3[part, TT * g:TT * g + TT, :, :].rearrange("p n g c -> p n (g c)")
                        act.dma_start(dst, view).then_inc(stats_in, 16)

            def merged_high(n):
                d = ysteps(n)
                act.wait_ge(merged, d + 1)
                nc.scalar.copy(mrg_hi[:, d, :], ysum[:, d % 2, :]).then_inc(mrg_hi_ready, 1)

            for s in range(NS):
                if s:
                    take_step(s - 1)
                if s + 2 < NS:
                    highs(s + 2)
                if s and step_kind(s - 1) == "y":
                    merged_high(s - 1)
                if s == 2 * OUT_AT - 3:
                    for k in range(4):
                        wo_highs(k)
                if s >= NS - 2:
                    for k in (4, 5) if s == NS - 2 else (6, 7):
                        wo_highs(k)
                if s - 1 >= 0:
                    for n in gated_in(s - 1):
                        w, c = GATED[n]
                        if w == "a":
                            act.wait_ge(dil_gated, c + 1)
                        else:
                            act.wait_ge(misc_taken, [m[1:] for m in MISC].index(("b", c)) + 1)
                        t = c if w == "a" else 2 + c
                        nc.scalar.copy(gat_hi[:, t, :], zf[:, t, :]).then_inc(gated_hi, 1)
                if s in TURNS:
                    take_turns(HEADS[TURNS[s]])
                for g in range(NDIL):
                    if s == scores_slot(HU * g + 3) + 1:
                        store_stats(g)
                if s == COEF - 1:
                    load_stats()
                if s == COEF:
                    act.wait_ge(gdif_ready, 1)
                    nc.scalar.activation(gexp[:], gdif[:], ACT.Exp).then_inc(gexp_ready, 1)
                if s in SCORES:
                    exps(HEADS[SCORES[s]])
            merged_high(NS - 1)

            for i in range(TT):
                for e in range(2):
                    act.wait_ge(res_added, 2 * i + e + 1)
                    nc.scalar.activation(ps[:, OUT_BANKS[2 * i + e], :], res[:, i % 2, 512 * e:512 * e + 512],
                                         ACT.Square, accum_out=ss[:, 4 + 2 * i + e:5 + 2 * i + e]).then_inc(res_squared, 1)
                act.wait_ge(out_var, i + 1)
                nc.scalar.activation(rstd[:, 4 + i:5 + i], rvar[:, 4 + i:5 + i], ACT.Sqrt).then_inc(out_rstd, 1)

        @block.vector
        def _(dve):
            chain = [0]

            def link(ins):
                ins.then_inc(dve_chain, 1)
                chain[0] += 1
                dve.wait_ge(dve_chain, chain[0])

            dve.wait_ge(vecs_turned, 1)
            link(nc.vector.tensor_copy(gb[:], ps[:, 7, 0:24]))
            nc.vector.tensor_scalar(hbias[:], gb[:, 8:24], 0.5, None, ALU.mult).then_inc(gb_ready, 1)

            def scale_rows(i):
                dve.wait_ge(rstd_ready, i + 1)
                nc.vector.tensor_scalar(xs[:, i, :], xs[:, i, :], rstd[:, i:i + 1], None,
                                        ALU.mult).then_inc(x_scaled, 1)

            for i in range(TT):
                dve.wait_ge(squared, i + 1)
                link(nc.vector.tensor_scalar(var[:, i:i + 1], ss[:, i:i + 1], 1.0 / D, EPS, ALU.mult, ALU.add))
                nc.vector.reciprocal(rvar[:, i:i + 1], var[:, i:i + 1]).then_inc(var_ready, 1)
                if i:
                    scale_rows(i - 1)
            scale_rows(TT - 1)
            for k in range(KT_D):
                dve.wait_ge(hT_hi_ready, k + 1)
                nc.vector.scalar_tensor_tensor(out=hT_lo[:, k, :], in0=ps[:, k, :], scalar=gb[:, k:k + 1],
                                               in1=hT_hi[:, k, :].bitcast(F32), op0=ALU.mult,
                                               op1=ALU.subtract).then_inc(hT_lo_ready, 1)

            def wo_lows(k):
                dve.wait_ge(wo_hi_ready, k + 1)
                nc.vector.tensor_tensor(wo("lo", k), raw_out(k), wo("hi", k).bitcast(F32),
                                        ALU.subtract).then_inc(wo_lo_ready, 1)

            def take_step(n):
                kind, u, j = step_kind(n), n // 6, n % 2
                if kind == "k":
                    dve.wait_ge(projected, n + 1)
                    if u >= 2:
                        dve.wait_ge(scored, HEADS[HU * (u - 1)].s0)
                    nc.vector.tensor_copy(residue_major(UNITS[u], KTs[:, u % 2, j, :]),
                                          residue_order(UNITS[u], ps[:, pbank(n), :])).then_inc(proj_taken[pbank(n)], 1)
                elif kind == "z":
                    z = zf[:, n - NZ0, :]
                    dve.wait_ge(z_tanh, n - NZ0 + 1)
                    nc.vector.scalar_tensor_tensor(out=z, in0=z, scalar=1.0, in1=ps[:, pbank(n), :],
                                                   op0=ALU.add, op1=ALU.mult).then_inc(proj_taken[pbank(n)], 1)

            def take_misc(m, what, at):
                dve.wait_ge(misc_ready, m + 1)
                src = ps[:, MB, :]
                if what == "a":
                    c, g = at
                    acc = dil_T[:, c, :]
                    if g == 0:
                        nc.vector.tensor_copy(acc, src).then_inc(misc_taken, 1)
                    else:
                        dve.wait_ge(misc_taken, m)
                        acc = residue_order(g, acc)
                        nc.vector.tensor_tensor(acc, residue_major(g, src), acc, ALU.add).then_inc(misc_taken, 1)
                else:
                    z = zf[:, 2 + at, :]
                    proj_taken_wait(dve, NZ0 + 2 + at)
                    nc.vector.tensor_tensor(z, src, z, ALU.mult).then_inc(misc_taken, 1)

            def gate_dilated(c):
                n = GATED.index(("a", c))
                m = [w == "a" and at == (c, NDIL - 1) for _, w, at in MISC].index(True)
                dve.wait_ge(misc_taken, m + 1)
                proj_taken_wait(dve, NZ0 + c)
                nc.vector.tensor_tensor(zf[:, c, :], dil_T[:, c, :], zf[:, c, :], ALU.mult).then_inc(dil_gated, 1)

            def gated_lows(n):
                w, c = GATED[n]
                t = c if w == "a" else 2 + c
                dve.wait_ge(gated_hi, n + 1)
                nc.vector.tensor_tensor(gat_lo[:, t, :], zf[:, t, :], gat_hi[:, t, :].bitcast(F32),
                                        ALU.subtract).then_inc(gated_lo, 1)

            def take_turns(h):
                for f in range(h.tfills):
                    if (h.t0 + f) % 2 == 1:
                        dve.wait_ge(turned, h.t0 + f + 1)
                        if h.n >= 2:
                            dve.wait_ge(valued, h.n - 1)
                        n = P * len(h.blocks[4 * f:4 * f + 4])
                        nc.vector.tensor_copy(probsT[:, h.n % 2, 512 * f:512 * f + n],
                                              ps[:, TB + 1, 0:n]).then_inc(turn_taken[1], 1)

            def mask_fill(h, f):
                lo, hi, _ = h.fills[f]
                dve.wait_ge(scored, h.s0 + f + 1)
                if h.n >= 2 and f == 0:
                    last = HEADS[h.n - 2]
                    dve.wait_ge(turned, last.t0 + last.tfills)
                src = ps[:, SB + (h.s0 + f) % 2, lo:hi]
                at = pfill(h.kind, f)
                dst = probs[:, h.n % 2, at + lo:at + hi]
                if h.kind == FULL:
                    dist = d_full[:, 512 - hi:512]
                elif h.kind == BAND:
                    dist = d_band[:, lo:hi]
                else:
                    dist = (d_quad if h.kind == QUAD else d_hex)[:, :].unsqueeze(1).broadcast_to([P, TT, P])
                    dst, src = (t.rearrange("p (i c) -> p i c", i=TT) for t in (dst, src))
                nc.vector.scalar_tensor_tensor(out=dst, in0=dist, scalar=SLOPE[h.n], in1=src, op0=ALU.mult,
                                               op1=ALU.subtract).then_inc(masked, 1)

            def min_rows(h, k):
                i, n, f = h.minima[k]
                dve.wait_ge(masked, h.s0 + f + 1)
                at, w = h.rows[i]
                src = probs[:, h.n % 2, at:at + n * w].rearrange("p (i c) -> p i c", i=n)
                nc.vector.tensor_reduce(nmin(h, i, n), src, AX.X, ALU.min).then_inc(min_ready, 1)

            def softmax_in(h):
                k = 0
                for f in range(len(h.fills)):
                    mask_fill(h, f)
                    while k < len(h.minima) and h.minima[k][2] < f:
                        min_rows(h, k)
                        k += 1
                while k < len(h.minima):
                    min_rows(h, k)
                    k += 1

            def take_values(h):
                dve.wait_ge(valued, h.n + 1)
                src = ps[:, PVB, 0:UW].rearrange("p (t c) -> p t c", t=TT)
                if h.unit < NDIL:
                    dst = o_dil[:, h.unit, :, HD * h.local:HD * h.local + HD]
                    nc.vector.tensor_copy(dst, src).then_inc(values_taken, 1)
                else:
                    n = h.n - NDIL * HU
                    dve.wait_ge(exp_ready, TT * (h.n + 1))
                    link(nc.vector.reciprocal(frec[:, n, :], fsum[:, n, :]))
                    nc.vector.tensor_tensor(o_full[:, :, HD * n:HD * n + HD], src,
                                            frec[:, n, :].unsqueeze(2).broadcast_to([P, TT, HD]),
                                            ALU.mult).then_inc(values_taken, 1)

            def coef_begin():
                dve.wait_ge(stats_in, 16 * NDIL)
                m = [stats3[:, :, g, 0:HU] for g in range(NDIL)]
                link(nc.vector.tensor_tensor(gmin[:], m[0], m[1], ALU.min))
                link(nc.vector.tensor_tensor(gmin[:], gmin[:], m[2], ALU.min))
                nc.vector.tensor_tensor(gdif[:], gmin[:].unsqueeze(2).broadcast_to([P, NDIL * TT, NDIL, HU]),
                                        stats3[:, :, :, 0:HU], ALU.subtract).then_inc(gdif_ready, 1)

            def coef_end():
                dve.wait_ge(gexp_ready, 1)
                link(nc.vector.tensor_tensor(gsum[:], gexp[:], stats3[:, :, :, HU:2 * HU], ALU.mult))
                link(nc.vector.tensor_tensor(gtot[:], gsum[:, :, 0, :], gsum[:, :, 1, :], ALU.add))
                link(nc.vector.tensor_tensor(gtot[:], gtot[:], gsum[:, :, 2, :], ALU.add))
                link(nc.vector.reciprocal(grec[:], gtot[:]))
                for g in range(NDIL):
                    r = slice(TT * g, TT * g + TT)
                    last = nc.vector.tensor_tensor(coef[:, r, :], gexp[:, r, g, :], grec[:, r, :], ALU.mult)
                    link(last)

            def scale_group(g):
                dve.wait_ge(values_taken, HU * (g + 1))
                o = o_dil[:, g, :, :].rearrange("p t (h c) -> p (t h) c", c=HD)
                c = coef[:, TT * g:TT * g + TT, :].rearrange("p t h -> p (t h)")
                nc.vector.tensor_tensor(o, o, c.unsqueeze(2).broadcast_to([P, TT * HU, HD]),
                                        ALU.mult).then_inc(o_scaled, 1)

            def merge(n):
                d, j = ysteps(n), n % 2
                dve.wait_ge(projected, n + 1)
                proj_taken_wait(dve, n - 2)
                proj_taken_wait(dve, n - 4)
                if d >= 1:
                    dve.wait_ge(mrg_hi_ready, d)
                link(nc.vector.scalar_tensor_tensor(out=ysum[:, 0, :] if d % 2 == 0 else ysum[:, 1, :],
                                                    in0=gate[:, j, :], scalar=1.0, in1=ps[:, ybank(n), :],
                                                    op0=ALU.add, op1=ALU.mult))
                g = gate[:, 2 + j, :]
                nc.vector.scalar_tensor_tensor(out=g, in0=g, scalar=1.0, in1=ps[:, ybank(n) + 1, :], op0=ALU.add,
                                               op1=ALU.mult).then_inc(y_taken, 1)
                dve.wait_ge(y_taken, d + 1)
                acc = ysum[:, d % 2, :]
                nc.vector.tensor_tensor(acc, acc, g, ALU.add).then_inc(merged, 1)
                dve.wait_ge(mrg_hi_ready, d + 1)
                nc.vector.tensor_tensor(mrg_lo[:, d, :], acc, mrg_hi[:, d, :].bitcast(F32),
                                        ALU.subtract).then_inc(mrg_lo_ready, 1)

            dve.wait_ge(consts_ready, 2)
            apart = d_hex[:].bitcast(I32)
            link(nc.vector.tensor_scalar(apart, apart, 3, None, ALU.bitwise_and))
            link(nc.vector.tensor_scalar(d_hex[:], apart, 1.0, BIG, ALU.min, ALU.mult))
            link(nc.vector.tensor_tensor(d_hex[:], d_hex[:], d_quad[:], ALU.max))
            for s in range(NS):
                if s:
                    take_step(s - 1)
                if s and step_kind(s - 1) == "y":
                    merge(s - 1)
                if s == 2 * OUT_AT - 3:
                    for k in range(4):
                        wo_lows(k)
                if s >= NS - 2:
                    for k in (4, 5) if s == NS - 2 else (6, 7):
                        wo_lows(k)
                if s == COEF + 1:
                    coef_end()
                if COEF < s <= COEF + NDIL:
                    scale_group(s - COEF - 1)
                if s == COEF:
                    coef_begin()
                for m, (slot, what, at) in enumerate(MISC):
                    if slot == s:
                        take_misc(m, what, at)
                if s in VALUES:
                    take_values(HEADS[VALUES[s]])
                if s in TURNS:
                    take_turns(HEADS[TURNS[s]])
                if s in SCORES:
                    softmax_in(HEADS[SCORES[s]])
                if s in GATED_A:
                    gate_dilated(GATED_A[s])
                for n in gated_in(s - 1):
                    gated_lows(n)
            merge(NS - 1)

            dve.wait_ge(fg_in, 16)
            for i in range(TT):
                dve.wait_ge(res_in[i % 2], 16 * (i // 2 + 1))
                r = res[:, i % 2, :]
                for e in range(2):
                    half = r[:, 512 * e:512 * e + 512]
                    dve.wait_ge(out_ready, 2 * i + e + 1)
                    nc.vector.scalar_tensor_tensor(out=half, in0=ps[:, OUT_BANKS[2 * i + e], :], scalar=0.25,
                                                   in1=half, op0=ALU.mult, op1=ALU.add).then_inc(res_added, 1)
                dve.wait_ge(res_squared, 2 * i + 2)
                a = 4 + 2 * i
                link(nc.vector.tensor_tensor(var[:, 4 + i:5 + i], ss[:, a:a + 1], ss[:, a + 1:a + 2], ALU.add))
                link(nc.vector.tensor_scalar(var[:, 4 + i:5 + i], var[:, 4 + i:5 + i], 1.0 / D, EPS,
                                             ALU.mult, ALU.add))
                nc.vector.reciprocal(rvar[:, 4 + i:5 + i], var[:, 4 + i:5 + i]).then_inc(out_var, 1)
                dve.wait_ge(out_rstd, i + 1)
                nc.vector.scalar_tensor_tensor(out=r, in0=r, scalar=rstd[:, 4 + i:5 + i], in1=fg[:], op0=ALU.mult,
                                               op1=ALU.mult).then_inc(out_done, 1)


_INS = ["x", "norm_g", "w_in", "b_merge", "w_pa", "w_pb", "w_out", "final_g"]
_FLAT = {"w_in", "w_pa", "w_pb", "w_out"}


def kernel(**inputs):
    import concourse.bacc as bacc
    from concourse.bass_utils import run_bass_kernel_spmd

    nc = bacc.Bacc("TRN2", target_bir_lowering=False, num_devices=1)
    arrays, args = {}, []
    for name in _INS:
        a = np.ascontiguousarray(inputs[name])
        if name in _FLAT:
            a = a.reshape(a.shape[1:])
        arrays[f"in_{name}"] = a
        args.append(nc.dram_tensor(f"in_{name}", a.shape, mybir.dt.from_np(a.dtype), kind="ExternalInput").ap())
    out = nc.dram_tensor("out_0", (1, SEQ, D), F32, kind="ExternalOutput").ap()
    hybrid_layer_program(nc, *args, out)
    r = run_bass_kernel_spmd(nc, [arrays], core_ids=[0])
    return r.results[0]["out_0"]
```

```python
from contextlib import ExitStack

import concourse.bass as bass
from concourse import mybir
import numpy as np

F32 = mybir.dt.float32
F32R = mybir.dt.float32r
I32 = mybir.dt.int32
ALU = mybir.AluOpType
ACT = mybir.ActivationFunctionType
AX = mybir.AxisListType

P = 128
SEQ = 512
D = 1024
TT = SEQ // P
KT_D = D // P
HD = 64
HU = 4
UW = HU * HD
EPS = 1e-6
BIG = 1e32

BAND, QUAD, HEX, FULL = range(4)
UNITS = [BAND, QUAD, HEX, FULL, FULL]
STACKED = (BAND, FULL)
NU = len(UNITS)
NH = NU * HU
NDIL = 3
DIL = [1, 4, 16]
C_A = NDIL * 3 * UW
C_ZA = C_A
C_B = C_ZA + UW
C_ZB = C_B + 3 * 2 * UW
C_RA = C_ZB + 2 * UW
C_RB = C_RA + D


def slopes(n):
    return [float(np.float32(2.0 ** (-8.0 * (i + 1) / n))) for i in range(n)]


SLOPE = slopes(NDIL * HU) + slopes(2 * HU)

CHUNKS = []
for u, kind in enumerate(UNITS):
    q = u * 3 * UW if u < NDIL else C_B + (u - NDIL) * UW
    w = UW if u < NDIL else 2 * UW
    CHUNKS += [("k", q + w), ("q", q), ("v", q + 2 * w)] if u == 0 else [("v", q + 2 * w), ("k", q + w), ("q", q)]
CHUNKS += [("z", C_ZA), ("z", C_ZB), ("z", C_ZB + UW)]
NZ0 = 2 * 3 * NU
NR0 = NZ0 + 6
ND = D // P
for j in range(ND // 2):
    CHUNKS += [("ra", C_RA + 256 * j), ("rb", C_RB + 256 * j), ("y", 256 * j)]
NS = 2 * len(CHUNKS)
OUT_AT = len(CHUNKS) - 3
LOADS = [("w", c) for c in range(OUT_AT)] + [("out", 0), ("out", 1)] + \
        [("w", c) for c in range(OUT_AT, len(CHUNKS))] + [("out", 2), ("out", 3)]
NRAW = 3
WARM = 14
NRING = 4
LOAD_OF = {item: n for n, item in enumerate(LOADS)}


def step_kind(n):
    return CHUNKS[n // 2][0]


def unit_step(u, kind, j):
    return 2 * [c[0] for c in CHUNKS[:3 * (u + 1)]].index(kind, 3 * u) + j


def stacks_before(n):
    return 2 * sum(1 for m in range(n) if stacks(m))


def k_stacks_before(n):
    return 2 * sum(1 for m in range(n) if stacks(m) and step_kind(m) == "k")


def pbank(n):
    return n % 2


def stacks(n):
    return n < 6 * NU and step_kind(n) in "kq" and UNITS[n // 6] in STACKED


def last_user(n):
    return max([m for m in range(n) if m % 2 == n % 2 and step_kind(m) != "y"], default=None)


def taken_count(n):
    return sum(1 for m in range(n + 1) if m % 2 == n % 2 and step_kind(m) != "y" and not stacks(m))


def ysteps(n):
    return sum(1 for m in range(n) if step_kind(m) == "y")


def fills(kind):
    if kind == FULL:
        return [(0, P * (i + 1), [(i, 0, 0, P * (i + 1))]) for i in range(TT)]
    if kind == BAND:
        return [(P, 512, [(0, P, 0, P), (1, 256, 0, 256)]),
                (0, 512, [(2, 0, P, 256), (3, 256, 2 * P, 256)])]
    return [(0, 512, [(i, P * i, P * i, P) for i in range(TT)])]


def prow(kind):
    if kind == FULL:
        return [(P * i * (i + 1) // 2, P * (i + 1)) for i in range(TT)]
    if kind == BAND:
        return [(P, P), (256, 256), (512, 256), (768, 256)]
    return [(P * i, P) for i in range(TT)]


def pfill(kind, f):
    if kind == FULL:
        return P * f * (f + 1) // 2
    return 512 * f


def blocks(kind):
    out = []
    for i, (at, n) in enumerate(prow(kind)):
        for b in range(n // P):
            kt = b if kind == FULL else (i - n // P + 1 + b if kind == BAND else i)
            out.append((i, kt, at + P * b))
    return sorted(out, key=lambda b: b[1]) if kind == FULL else out


T_KEYS = []
for _kt in range(TT):
    T_KEYS.append((sum(n for _, n in T_KEYS), max(SEQ - P * _kt, 256)))
T_ZERO = T_KEYS[-1][0]
T_FILL = 4 * P
T_WIDE = 3 * T_FILL


def minima(kind):
    if kind == FULL:
        return [(i, 1, i) for i in range(TT)]
    if kind == BAND:
        return [(0, 1, 0), (1, 1, 0), (2, 2, 1)]
    return [(0, TT, 0)]


GROUPS = [(i, 512 * e, 512) for i in range(TT) for e in range(2)]
GROUPS[-1:] = [(TT - 1, 512, 256), (TT - 1, 768, 256)]


def groups_of(i):
    return [g for g, (tile, _, _) in enumerate(GROUPS) if tile == i]


class Head:
    pass


HEADS = []
_s = _m = _t = 0
for h in range(NH):
    x = Head()
    x.n, x.unit, x.kind = h, h // HU, UNITS[h // HU]
    x.local, x.pair, x.part = h % HU, (h % HU) // 2, HD * (h % 2)
    x.fills, x.rows, x.blocks, x.minima = fills(x.kind), prow(x.kind), blocks(x.kind), minima(x.kind)
    x.s0, x.m0, x.t0 = _s, _m, _t
    x.tfills = -(-len(x.blocks) // 4)
    _s, _m, _t = _s + len(x.fills), _m + len(x.minima), _t + x.tfills
    HEADS.append(x)


TURN_BANK = []
for x in HEADS:
    x.turn_banks = [0, 1, 2] if x.kind == FULL else [(x.t0 + f) % 2 for f in range(x.tfills)]
    TURN_BANK += x.turn_banks
assert TURN_BANK.index(2) % 2 == 0


def bank_turns(b, fill):
    return TURN_BANK[:fill].count(b)


def scores_slot(h):
    return 6 * (h // HU + 1) + h % HU


SCORES = {scores_slot(h): h for h in range(NH)}
TURNS = {scores_slot(h) + 1: h for h in range(NH)}
VALUES = {scores_slot(h) + 2: h for h in range(NH)}

MISC = []
COEF = scores_slot(NDIL * HU + HU - 1) - 1
MISC += [(COEF + 3 + 2 * g + c, (c, g)) for g in range(NDIL) for c in range(2)]
LAST_MISC = MISC[-1][0]
GATED = [(LAST_MISC, "a", 0), (LAST_MISC, "b", 0), (LAST_MISC, "b", 1),
         (LAST_MISC + 1, "a", 1), (LAST_MISC + 1, "b", 2), (LAST_MISC + 2, "b", 3)]


def gated_in(slot):
    return [n for n, g in enumerate(GATED) if g[0] == slot]


def hybrid_layer_program(nc, x, norm_g, w_in, b_merge, w_pa, w_pb, w_out, final_g, out):
    stats_dram = nc.dram_tensor("stats_by_position", (SEQ, NDIL * 8), F32, kind="Internal").ap()
    top = ExitStack()
    with top:
        def sb(name, shape, dt, stack=top):
            return stack.enter_context(nc.sbuf_tensor(name, shape, dt))

        def sem(name):
            return top.enter_context(nc.semaphore(name))

        raw = sb("raw", [P, NRAW, KT_D * 256], F32)
        w_hi = sb("w_hi", [P, NRING, KT_D * P], F32R)
        w_lo = sb("w_lo", [P, NRING, KT_D * P], F32R)
        ostack = ExitStack()
        o_dil = sb("o_dil", [P, NDIL, TT, UW], F32, ostack)
        with ExitStack() as stack:
            V_odd = sb("V_odd", [P, TT, UW], F32, stack)
        V_split_odd = sb("V_split_odd", [P, TT, HU, 2, HD], F32R, ostack)
        ostack.close()
        gat_hi = sb("gat_hi", [P, 6, SEQ], F32R)
        gat_lo = sb("gat_lo", [P, 6, SEQ], F32R)
        d_quad = sb("d_quad", [P, P], F32)
        d_hex = sb("d_hex", [P, P], F32)
        ident = sb("ident", [P, P], F32)
        vecs = sb("vecs", [24, P], F32)
        gb = sb("gb", [P, 24], F32)
        hbias = sb("hbias", [P, 16], F32)
        ss = sb("ss", [P, TT], F32)
        out_ss = sb("out_ss", [P, len(GROUPS)], F32)
        unread = sb("unread", [P, 1], F32)
        var = sb("var", [P, TT], F32)
        rvar = sb("rvar", [P, TT], F32)
        mean = sb("mean", [P, len(GROUPS)], F32)
        rms = sb("rms", [P, TT], F32)
        rstd = sb("rstd", [P, 2 * TT], F32)

        dstack = ExitStack()
        d_full = sb("d_full", [P, 512], F32, dstack)
        d_band = sb("d_band", [P, 512], F32, dstack)
        dstack.close()
        fg = sb("fg", [P, D], F32)
        hstack = ExitStack()
        hT_hi = sb("hT_hi", [P, KT_D, SEQ], F32R, hstack)
        hT_lo = sb("hT_lo", [P, KT_D, SEQ], F32R, hstack)
        xstack = ExitStack()
        xs = sb("xs", [P, TT, D], F32, xstack)
        squares = sb("squares", [P, TT, D], F32, xstack)
        xstack.close()
        astack = ExitStack()
        probs = sb("probs", [P, 2, 1280], F32, astack)
        fstack = ExitStack()
        KTf = sb("KTf", [P, 2, 4 * SEQ], F32, fstack)
        QTf = sb("QTf", [P, 2, 2 * SEQ], F32, fstack)
        fstack.close()
        KTs = sb("KTs", [P, HU, 2, SEQ], F32R, astack)
        QTs = sb("QTs", [P, HU, SEQ], F32R, astack)
        with ExitStack() as stack:
            V_even = sb("V_even", [P, TT, UW], F32, stack)
        V_split_even = sb("V_split_even", [P, TT, HU, 2, HD], F32R, astack)
        with ExitStack() as stack:
            probsT = sb("probsT", [P, 7 * P], F32, stack)
        pT_hi = sb("pT_hi", [P, T_WIDE], F32R, astack)
        pT_lo = sb("pT_lo", [P, T_WIDE], F32R, astack)
        o_lows = sb("o_lows", [HD, SEQ], F32, astack)
        o_full = sb("o_full", [P, 4, SEQ], F32, astack)
        zf = sb("zf", [P, 6, SEQ], F32, astack)
        dil_T = sb("dil_T", [P, 2, SEQ], F32, astack)
        stats = sb("stats", [P, TT, NDIL * 8], F32, astack)
        stats3 = sb("stats3", [P, NDIL * TT, NDIL, 8], F32, astack)
        gmin = sb("gmin", [P, NDIL * TT, HU], F32, astack)
        gdif = sb("gdif", [P, NDIL * TT, NDIL, HU], F32, astack)
        gexp = sb("gexp", [P, NDIL * TT, NDIL, HU], F32, astack)
        gsum = sb("gsum", [P, NDIL * TT, NDIL, HU], F32, astack)
        gtot = sb("gtot", [P, NDIL * TT, HU], F32, astack)
        grec = sb("grec", [P, NDIL * TT, HU], F32, astack)
        coef = sb("coef", [P, NDIL * TT, HU], F32, astack)
        fmin = sb("fmin", [P, 2 * HU, TT], F32, astack)
        fsum = sb("fsum", [P, 2 * HU, TT], F32, astack)
        frec = sb("frec", [P, 2 * HU, TT], F32, astack)
        astack.close()
        hstack.close()
        wo_b_hi = sb("wo_b_hi", [P, 3, D], F32R)
        wo_b_lo = sb("wo_b_lo", [P, 3, D], F32R)
        res = sb("res", [P, 2, D], F32)
        wstack = ExitStack()
        gate = sb("gate", [P, 4, SEQ], F32, wstack)
        wstack.close()
        weighted = sb("weighted", [P, 2, D], F32)
        wo_a_hi = sb("wo_a_hi", [P, 5, D], F32R)
        wo_a_lo = sb("wo_a_lo", [P, 5, D], F32R)
        mrg_hi = sb("mrg_hi", [P, ND, SEQ], F32R)
        mrg_lo = sb("mrg_lo", [P, ND, SEQ], F32R)
        ysum = sb("ysum", [P, 2, SEQ], F32)

        ps = top.enter_context(nc.psum_tensor("ps", [P, 8, 512], F32))
        def ybank(n):
            return SB if ysteps(n) % 2 == 0 else TB

        SB, TB, PVB, MB = 2, 4, 6, 7
        TURN_BANKS = [TB, TB + 1, MB]
        OUT_BANKS = [6, 7, 0, 1, 2, 3, 4, 5, 6]

        x_in = [sem(f"x_in{i}") for i in range(TT)]
        vec_in = sem("vec_in")
        fg_in = sem("fg_in")
        raw_in = [sem(f"raw_in{i}") for i in range(NRAW)]
        first_half_in = [sem(f"first_half_in{i}") for i in range(2)]
        const_step = sem("const_step")
        consts_ready = sem("consts_ready")
        squared = sem("squared")
        act_chain = sem("act_chain")
        dve_chain = sem("dve_chain")
        var_ready = sem("var_ready")
        rstd_ready = sem("rstd_ready")
        x_scaled = sem("x_scaled")
        vecs_turned = sem("vecs_turned")
        gb_ready = sem("gb_ready")
        x_turned = sem("x_turned")
        hT_hi_ready = sem("hT_hi_ready")
        hT_lo_ready = sem("hT_lo_ready")
        hi_ready = sem("hi_ready")
        lo_ready = sem("lo_ready")
        wo_hi_ready = sem("wo_hi_ready")
        wo_lo_ready = sem("wo_lo_ready")
        projected = sem("projected")
        proj_taken = [sem(f"proj_taken{b}") for b in range(2)]
        split_hi = sem("split_hi")
        k_low = sem("k_low")
        stacked = sem("stacked")
        z_tanh = sem("z_tanh")
        misc_ready = sem("misc_ready")
        misc_taken = sem("misc_taken")
        scored = sem("scored")
        masked = sem("masked")
        min_ready = sem("min_ready")
        exp_ready = sem("exp_ready")
        turned = sem("turned")
        turn_taken = [sem(f"turn_taken{b}") for b in range(3)]
        valued = sem("valued")
        v_split_hi = sem("v_split_hi")
        turned_hi = sem("turned_hi")
        frec_ready = sem("frec_ready")
        normed = sem("normed")
        o_lows_ready = sem("o_lows_ready")
        values_taken = sem("values_taken")
        moba_gated = sem("moba_gated")
        stats_out = sem("stats_out")
        stats_in = sem("stats_in")
        gdif_ready = sem("gdif_ready")
        gexp_ready = sem("gexp_ready")
        o_scaled = sem("o_scaled")
        dil_gated = sem("dil_gated")
        gated_hi = sem("gated_hi")
        gated_lo = sem("gated_lo")
        y_taken = sem("y_taken")
        merged = sem("merged")
        mrg_hi_ready = sem("mrg_hi_ready")
        mrg_lo_ready = sem("mrg_lo_ready")
        out_ready = sem("out_ready")
        res_in = [sem(f"res_in{i}") for i in range(2)]
        res_added = sem("res_added")
        res_squared = sem("res_squared")
        out_rms = sem("out_rms")
        out_done = sem("out_done")
        out_mean = sem("out_mean")
        weighed = sem("weighed")
        stored = [sem(f"stored{i}") for i in range(2)]

        w_in_t = w_in.rearrange("(k p) c -> p k c", p=P)
        w_pa_t = w_pa.rearrange("(k p) c -> p k c", p=P)
        w_pb_t = w_pb.rearrange("(k p) c -> p k c", p=P)
        w_out_t = w_out.rearrange("(k p) c -> p k c", p=P)
        x_t = x.rearrange("b (n p) d -> p (b n) d", p=P)
        out_t = out.rearrange("b (n p) d -> p (b n) d", p=P)

        def raw_waits(item, half=0):
            if item == ("w", 0):
                return first_half_in[half], 16
            n = LOAD_OF[item]
            count = 0
            for m in range(n % NRAW, n + 1, NRAW):
                k, c = LOADS[m]
                count += 0 if m == 0 else 32 if k == "w" and CHUNKS[c][0] == "y" else 16
            return raw_in[n % NRAW], count

        def halves_before(n):
            return (2 * sum(1 for k, _ in LOADS[:n + 1] if k == "w"),
                    2 * sum(1 for k, _ in LOADS[:n + 1] if k == "out"))

        def raw_half(n):
            slot = LOAD_OF[("w", n // 2)] % NRAW
            kt = 6 if step_kind(n) == "y" else KT_D
            return raw[:, slot, 0:kt * 256].rearrange("p (k c) -> p k c", k=kt)[:, :, P * (n % 2):P * (n % 2) + P], kt

        def ring(t, n, kt):
            return t[:, n % NRING, 0:kt * P].rearrange("p (k c) -> p k c", k=kt)

        def raw_out(k):
            return raw[:, LOAD_OF[("out", k // 2)] % NRAW, D * (k % 2):D * (k % 2) + D]

        def wo(part, k):
            a, b = (wo_a_hi, wo_b_hi) if part == "hi" else (wo_a_lo, wo_b_lo)
            return a[:, k, :] if k < 5 else b[:, k - 5, :]

        def pair_ring(t, n):
            at = n // 2 * 2 % NRING
            return t[:, at:at + 2, :]

        def rows_of(kind, t, i):
            if kind in (QUAD, HEX):
                return t.rearrange("p (i r) -> p r i", r=TT)[:, i, :]
            return t[:, P * i:P * i + P]

        def residue_order(kind, t):
            return t if kind in (BAND, FULL) else t.rearrange("p (i r) -> p r i", r=TT)

        def residue_major(kind, t):
            return t if kind in (BAND, FULL) else t.rearrange("p (r i) -> p r i", r=TT)

        def nmin(h, i, n=1):
            if h.unit < NDIL:
                return stats[:, i:i + n, 8 * h.unit + h.local]
            return fmin[:, h.n - NDIL * HU, i:i + n]

        def row_sum(h, i):
            if h.unit < NDIL:
                return stats[:, i, 8 * h.unit + HU + h.local:8 * h.unit + HU + h.local + 1]
            return fsum[:, h.n - NDIL * HU, i:i + 1]

        def split_values(u):
            return V_split_odd if u % 2 else V_split_even

        def v_steps_before(n):
            return sum(1 for m in range(n) if step_kind(m) == "v" and UNITS[m // 6] == FULL)

        def turned_columns(t, f):
            t = t[:, T_FILL * f:T_FILL * f + T_FILL]
            return t if f < 2 else t.rearrange("p (a b c) -> p a b c", a=2, b=2)[:, :, 0, :]

        def halves(e):
            return slice(HD * e, HD * e + HD), slice(HD - HD * e, 2 * HD - HD * e)

        def before_in_place(n):
            last = HEADS[HU * (n // 6 - 1) + 2 * (n % 2) + 1]
            return last.s0 + len(last.fills)

        def turn_taken_wait(eng, fill):
            b = TURN_BANK[fill]
            eng.wait_ge(turn_taken[b], bank_turns(b, fill + 1))

        def proj_taken_wait(eng, n):
            if stacks(n) and step_kind(n) == "k":
                eng.wait_ge(k_low, k_stacks_before(n) + 2)
            elif stacks(n):
                eng.wait_ge(stacked, stacks_before(n) + 2)
            else:
                eng.wait_ge(proj_taken[pbank(n)], taken_count(n))

        block = top.enter_context(nc.Block())

        @block.sync
        def _(sp):
            for i in range(TT):
                sp.dma_start(xs[:, i, :], x_t[:, i, :]).then_inc(x_in[i], 16)
            for n, (k, c) in enumerate(LOADS):
                if n >= NRAW:
                    ring_n, out_n = halves_before(n - NRAW)
                    sp.wait_ge(hi_ready, ring_n)
                    sp.wait_ge(lo_ready, ring_n)
                    if out_n:
                        sp.wait_ge(wo_hi_ready, out_n)
                        sp.wait_ge(wo_lo_ready, out_n)
                slot, s = raw[:, n % NRAW, :], raw_in[n % NRAW]
                if k == "out":
                    sp.dma_start(slot.rearrange("p (k c) -> p k c", k=2), w_out_t[:, 2 * c:2 * c + 2, :]).then_inc(s, 16)
                elif CHUNKS[c][0] == "y":
                    at = CHUNKS[c][1]
                    dst = slot[:, 0:6 * 256].rearrange("p (k c) -> p k c", k=6)
                    sp.dma_start(dst[:, 0:2, :], w_pa_t[:, :, at:at + 256]).then_inc(s, 16)
                    sp.dma_start(dst[:, 2:6, :], w_pb_t[:, :, at:at + 256]).then_inc(s, 16)
                else:
                    at = CHUNKS[c][1]
                    dst = slot.rearrange("p (k c) -> p k c", k=KT_D)
                    if n == 0:
                        sp.dma_start(dst[:, :, 0:P], w_in_t[:, :, at:at + P]).then_inc(first_half_in[0], 16)
                        sp.dma_start(dst[:, :, P:256], w_in_t[:, :, at + P:at + 256]).then_inc(first_half_in[1], 16)
                    else:
                        sp.dma_start(dst, w_in_t[:, :, at:at + 256]).then_inc(s, 16)
            sp.wait_ge(masked, _s)
            sp.dma_start(fg[:, :], final_g.partition_broadcast(P)).then_inc(fg_in, 16)
            sp.wait_ge(projected, NS - 2)
            for i in range(2):
                sp.dma_start(res[:, i, :], x_t[:, i, :]).then_inc(res_in[i], 16)
            for i in range(TT):
                for e, g in ((0, groups_of(i)[0]), (1, groups_of(i)[-1])):
                    half = slice(512 * e, 512 * e + 512)
                    sp.wait_ge(out_done, g + 1)
                    sp.dma_start(out_t[:, i, half], weighted[:, i % 2, half]).then_inc(stored[i % 2], 16)
                if i + 2 < TT:
                    sp.wait_ge(res_squared, groups_of(i)[-1] + 1)
                    sp.wait_ge(weighed, groups_of(i)[-1] + 1)
                    sp.dma_start(res[:, i % 2, :], x_t[:, i + 2, :]).then_inc(res_in[i % 2], 16)
            for b in range(2):
                sp.wait_ge(stored[b], 16 * TT)

        @block.gpsimd
        def _(pool):
            steps = [0]

            def link(ins):
                ins.then_inc(const_step, 1)
                steps[0] += 1
                pool.wait_ge(const_step, steps[0])

            link(nc.gpsimd.memset(ident[:], 0.0))
            nc.gpsimd.affine_select(out=ident[:], in_=ident[:], compare_op=ALU.not_equal, fill=1.0, base=0,
                                    pattern=[[-1, P]], channel_multiplier=1).then_inc(consts_ready, 1)
            pool.wait_ge(consts_ready, 1)

            def lows(n):
                pool.wait_ge(hi_ready, n + 1)
                s, count = raw_waits(("w", n // 2), n % 2)
                pool.wait_ge(s, count)
                if n >= NRING:
                    pool.wait_ge(projected, n - 2)
                src, kt = raw_half(n)
                nc.gpsimd.tensor_tensor(ring(w_lo, n, kt), src, ring(w_hi, n, kt).bitcast(F32),
                                        ALU.subtract).then_inc(lo_ready, 1)

            link(nc.gpsimd.iota(d_full[:], [[-1, 512]], base=384, channel_multiplier=1,
                                allow_small_or_imprecise_dtypes=True))
            link(nc.gpsimd.affine_select(out=d_full[:], in_=d_full[:], compare_op=ALU.is_ge, fill=BIG, base=384,
                                         pattern=[[-1, 512]], channel_multiplier=1))
            band = d_band[:].rearrange("p (a c) -> p a c", a=2)
            link(nc.gpsimd.iota(band, [[0, 2], [-1, 256]], base=P, channel_multiplier=1,
                                allow_small_or_imprecise_dtypes=True))
            link(nc.gpsimd.affine_select(out=band, in_=band, compare_op=ALU.is_ge, fill=BIG, base=P,
                                         pattern=[[0, 2], [-1, 256]], channel_multiplier=1))
            link(nc.gpsimd.affine_select(out=band, in_=band, compare_op=ALU.is_ge, fill=BIG, base=0,
                                         pattern=[[0, 2], [1, 256]], channel_multiplier=-1))
            link(nc.gpsimd.iota(d_quad[:], [[-4, P]], base=0, channel_multiplier=4,
                                allow_small_or_imprecise_dtypes=True))
            link(nc.gpsimd.affine_select(out=d_quad[:], in_=d_quad[:], compare_op=ALU.is_ge, fill=BIG, base=0,
                                         pattern=[[-1, P]], channel_multiplier=1))
            nc.gpsimd.iota(d_hex[:].bitcast(I32), [[-1, P]], base=0, channel_multiplier=1).then_inc(consts_ready, 1)
            pool.wait_ge(consts_ready, 2)
            pool.wait_ge(hi_ready, 1)
            pool.wait_ge(first_half_in[1], 16)
            src, kt = raw_half(1)
            nc.gpsimd.tensor_copy(ring(w_hi, 1, kt), src).then_inc(hi_ready, 1)
            pool.wait_ge(lo_ready, 1)

            def normalise(h):
                pool.wait_ge(frec_ready, h.n - NDIL * HU + 1)
                for i, (at, n) in enumerate(h.rows):
                    row = probs[:, h.n % 2, at:at + n]
                    nc.gpsimd.tensor_tensor(row, row, frec[:, h.n - NDIL * HU, i:i + 1].broadcast_to([P, n]),
                                            ALU.mult).then_inc(normed, 1)

            for n in range(1, NS):
                if n - 2 in TURNS and HEADS[TURNS[n - 2]].kind == FULL:
                    normalise(HEADS[TURNS[n - 2]])
                lows(n)

        @block.tensor
        def _(pe):
            pe.wait_ge(consts_ready, 1)
            for _ in range(WARM):
                pe.matmul(ps[:, 0, 0:P], ident[:, :], ident[:, :], start=True, stop=True)
            for i in range(TT):
                pe.wait_ge(x_scaled, i + 1)
                for k in range(KT_D):
                    if i == TT - 1 and k == 7:
                        pe.wait_ge(gb_ready, 1)
                    last = pe.transpose(ps[:, k, P * i:P * i + P], xs[:, i, P * k:P * k + P], ident[:, :])
                last.then_inc(x_turned, 1)
                if i == TT - 2:
                    pe.wait_ge(vec_in, 32)
                    pe.transpose(ps[:, 7, SEQ - 24:SEQ], vecs[:, :], ident[0:24, 0:24]).then_inc(vecs_turned, 1)

            def weights_wait(n):
                pe.wait_ge(hi_ready, n + 1)
                pe.wait_ge(lo_ready, n + 1)

            def term(out, k, kts, wh, wl, hh, hl, hh_count=0):
                if hh_count:
                    pe.wait_ge(hT_hi_ready, hh_count)
                pe.matmul(out, wh, hh, start=(k == 0), stop=False)
                pe.matmul(out, wl, hh, start=False, stop=False)
                if hh_count:
                    pe.wait_ge(hT_lo_ready, hh_count)
                return pe.matmul(out, wh, hl, start=False, stop=(k == kts - 1))

            def step_pieces(n):
                kind = step_kind(n)

                def start():
                    weights_wait(n)
                    if kind == "v":
                        weights_wait(n // 2 * 2 + 1)
                    if kind == "y":
                        if ysteps(n) == 0:
                            pe.wait_ge(gated_hi, 6)
                            pe.wait_ge(gated_lo, 6)
                            pe.wait_ge(masked, _s)
                            for b in range(2):
                                pe.wait_ge(turn_taken[b], bank_turns(b, _t))
                        if ysteps(n) >= 2:
                            pe.wait_ge(y_taken, ysteps(n) - 1)
                    elif last_user(n) is not None:
                        proj_taken_wait(pe, last_user(n))

                def column_tile(k):
                    if n == 1 and k == 0:
                        pe.wait_ge(hT_lo_ready, 2)
                    if n == 0 and k == 0:
                        pe.wait_ge(hT_lo_ready, 1)
                    last = term(ps[:, pbank(n), :], k, KT_D, ring(w_hi, n, KT_D)[:, k, :],
                                ring(w_lo, n, KT_D)[:, k, :], hT_hi[:, k, :], hT_lo[:, k, :],
                                hh_count=k + 1 if n == 0 else 0)
                    if k == KT_D - 1:
                        last.then_inc(projected, 1)

                def value_rows(i, ks):
                    kind_u = UNITS[n // 6]
                    t = 2 * (n % 2) + i
                    for k in ks:
                        hh, hl = (rows_of(kind_u, h[:, k, :], t) for h in (hT_hi, hT_lo))
                        wh, wl = (pair_ring(w, n)[:, :, P * k:P * k + P] for w in (w_hi, w_lo))
                        o = ps[:, pbank(n), UW * i:UW * i + UW].rearrange("p (j c) -> p j c", j=2)
                        pe.matmul(o, hh, wh, start=(k == 0), stop=False)
                        pe.matmul(o, hl, wh, start=False, stop=False)
                        last = pe.matmul(o, hh, wl, start=False, stop=(k == KT_D - 1))
                    if i == 1 and ks[-1] == KT_D - 1:
                        last.then_inc(projected, 1)

                def branches(ks):
                    for k in ks:
                        b = k >= 2
                        last = term(ps[:, ybank(n) + b, :], k - 2 * b, 4 if b else 2, ring(w_hi, n, 6)[:, k, :],
                                    ring(w_lo, n, 6)[:, k, :], gat_hi[:, k, :], gat_lo[:, k, :])
                    if ks[-1] == 5:
                        last.then_inc(projected, 1)

                if kind == "v":
                    pieces = [lambda i=i, k=k: value_rows(i, [k, k + 1]) for i in range(2) for k in range(0, KT_D, 2)]
                elif kind == "y":
                    pieces = [lambda k=k: branches([k, k + 1]) for k in range(0, 6, 2)]
                else:
                    pieces = [lambda k=k: column_tile(k) for k in range(KT_D)]
                first = pieces[0]
                pieces[0] = lambda: (start(), first())
                return pieces

            misc_begun, third_begun = [0], [0]

            def turn_misc(m, c, g):
                if m:
                    pe.wait_ge(misc_taken, m)
                if third_begun[0]:
                    pe.wait_ge(turn_taken[2], third_begun[0])
                misc_begun[0] += 1
                pe.wait_ge(o_scaled, g + 1)
                for t in range(TT):
                    last = pe.transpose(ps[:, MB, P * t:P * t + P], o_dil[:, g, t, P * c:P * c + P], ident[:, :])
                last.then_inc(misc_ready, 1)

            def scores(h, f):
                k_step, q_step = (unit_step(h.unit, kind, h.pair) for kind in "kq")
                if f == 0 and h.kind in STACKED:
                    pe.wait_ge(stacked, stacks_before(k_step) + h.local % 2 + 1)
                    pe.wait_ge(stacked, stacks_before(q_step) + h.local % 2 + 1)
                elif f == 0:
                    proj_taken_wait(pe, k_step)
                    proj_taken_wait(pe, q_step)
                if h.s0 + f >= 2:
                    pe.wait_ge(masked, h.s0 + f - 1)
                bank = ps[:, SB + (h.s0 + f) % 2, :]
                for i, at, k0, nk in h.fills[f][2]:
                    rows = slice(P * i, P * i + P)
                    if h.kind in STACKED:
                        nk = max(nk, 256)
                        for part in range(2):
                            last = pe.matmul(bank[:, at:at + nk], QTs[:, h.local, rows],
                                             KTs[:, h.local, part, k0:k0 + nk], start=(part == 0), stop=(part == 1))
                    else:
                        K, Q = (t[h.part:h.part + HD, h.pair, 0:SEQ] for t in (KTf, QTf))
                        last = pe.matmul(bank[:, at:at + nk], Q[:, rows], K[:, k0:k0 + nk], start=True, stop=True)
                last.then_inc(scored, 1)

            def turns(h, f):
                bank = h.turn_banks[f]
                before = bank_turns(bank, h.t0 + f)
                if before:
                    pe.wait_ge(turn_taken[bank], before)
                if bank == 2 and misc_begun[0]:
                    pe.wait_ge(misc_taken, misc_begun[0])
                third_begun[0] += bank == 2
                for b, (i, _, at) in enumerate(h.blocks[4 * f:4 * f + 4]):
                    if h.kind == FULL:
                        pe.wait_ge(normed, TT * (h.n - NDIL * HU) + i + 1)
                    else:
                        pe.wait_ge(exp_ready, TT * h.n + i + 1)
                    last = pe.transpose(ps[:, TURN_BANKS[bank], P * b:P * b + P],
                                        probs[:, h.n % 2, at:at + P], ident[:, :])
                last.then_inc(turned, 1)

            def values(h):
                for f in range(h.tfills):
                    turn_taken_wait(pe, h.t0 + f)
                if h.n:
                    pe.wait_ge(values_taken, h.n)
                for j in range(2):
                    proj_taken_wait(pe, unit_step(h.unit, "v", j))
                if h.kind == FULL:
                    for kt, (at, n) in enumerate(T_KEYS):
                        for t in (pT_hi, pT_lo):
                            last = pe.matmul(ps[:, PVB, SEQ - n:SEQ],
                                             split_values(h.unit)[:, kt, h.local, :, :].rearrange("p a c -> p (a c)"),
                                             t[:, at:at + n], start=(kt == 0 and t is pT_hi),
                                             stop=(kt == TT - 1 and t is pT_lo))
                    last.then_inc(valued, 1)
                    return
                V = V_odd if h.unit % 2 else V_even
                for i in range(TT):
                    mine = [(b, kt) for b, (q, kt, _) in enumerate(h.blocks) if q == i]
                    for b, kt in mine:
                        last = pe.matmul(ps[:, PVB, HD * i:HD * i + HD], probsT[:, P * b:P * b + P],
                                         V[:, kt, HD * h.local:HD * h.local + HD],
                                         start=((b, kt) == mine[0]), stop=((b, kt) == mine[-1]))
                last.then_inc(valued, 1)

            for s in range(NS):
                score, turn = [], []
                if s in SCORES:
                    h = HEADS[SCORES[s]]
                    score = [lambda h=h, f=f: scores(h, f) for f in range(len(h.fills))]
                if s in TURNS:
                    h = HEADS[TURNS[s]]
                    turn = [lambda h=h, f=f: turns(h, f) for f in range(h.tfills)]
                between = score[:2]
                misc = [lambda m=m, at=at: turn_misc(m, *at) for m, (slot, at) in enumerate(MISC) if slot == s]
                value = [lambda: values(HEADS[VALUES[s]])] if s in VALUES else []
                between += misc + value if score else [lambda: None] * 3 * len(value) + value + misc
                between += score[2:] + turn
                if score:
                    between += [lambda: None] * (KT_D - len(between))
                pieces = step_pieces(s)
                n, m = len(pieces), len(between)
                for i, piece in enumerate(pieces):
                    piece()
                    for other in between[m * i // n:m * (i + 1) // n]:
                        other()

            for i in range(TT):
                groups = groups_of(i)
                banks = [OUT_BANKS[g] for g in groups]
                if 2 in banks or 4 in banks:
                    pe.wait_ge(y_taken, ysteps(NS) - (4 in banks) * (ybank(NS - 1) != 4))
                if 0 in banks:
                    proj_taken_wait(pe, NS - 3)
                    proj_taken_wait(pe, NS - 4)
                if MB in banks:
                    pe.wait_ge(misc_taken, len(MISC))
                    pe.wait_ge(turn_taken[2], third_begun[0])
                    pe.wait_ge(values_taken, NH)
                order = [(k, g) for k in range(KT_D) for g in groups] if i == 0 else \
                        [(k, g) for g in groups for k in range(KT_D)]
                for k, g in order:
                    if g == 0:
                        pe.wait_ge(wo_lo_ready, k + 1)
                        pe.wait_ge(wo_hi_ready, k + 1)
                        pe.wait_ge(mrg_hi_ready, k + 1)
                        pe.wait_ge(mrg_lo_ready, k + 1)
                    if g == len(GROUPS) - 1 and k == 0:
                        pe.wait_ge(res_squared, 1)
                    _, at, n = GROUPS[g]
                    o, cols = ps[:, OUT_BANKS[g], 0:n], slice(at, at + n)
                    mh, ml = mrg_hi[:, k, P * i:P * i + P], mrg_lo[:, k, P * i:P * i + P]
                    pe.matmul(o, mh, wo("hi", k)[:, cols], start=(k == 0), stop=False)
                    pe.matmul(o, mh, wo("lo", k)[:, cols], start=False, stop=False)
                    last = pe.matmul(o, ml, wo("hi", k)[:, cols], start=False, stop=(k == KT_D - 1))
                    if k == KT_D - 1:
                        last.then_inc(out_ready, 1)

        @block.scalar
        def _(act):
            def highs(n):
                s, count = raw_waits(("w", n // 2), n % 2)
                act.wait_ge(s, count)
                if n == 2:
                    act.wait_ge(hi_ready, 2)
                if n >= NRING:
                    act.wait_ge(projected, n - 2)
                src, kt = raw_half(n)
                nc.scalar.copy(ring(w_hi, n, kt), src).then_inc(hi_ready, 1)

            def wo_highs(k):
                s, count = raw_waits(("out", k // 2))
                act.wait_ge(s, count)
                if k == 0:
                    act.wait_ge(gated_lo, 6)
                    act.wait_ge(gated_hi, 6)
                if k == 5:
                    act.wait_ge(projected, NS - 2)
                nc.scalar.copy(wo("hi", k), raw_out(k)).then_inc(wo_hi_ready, 1)

            act.dma_start(vecs[0:8, :], norm_g.rearrange("l (k p) -> (l k) p", p=P)).then_inc(vec_in, 16)
            act.dma_start(vecs[8:24, :], b_merge.rearrange("l (k p) -> (l k) p", p=P)).then_inc(vec_in, 16)
            act.wait_ge(consts_ready, 1)
            nc.scalar.activation(unread[:], ident[:, 0:1], ACT.Sqrt)
            for i in range(TT):
                act.wait_ge(x_in[i], 16)
                nc.scalar.activation(squares[:, i, :], xs[:, i, :], ACT.Square,
                                     accum_out=ss[:, i:i + 1]).then_inc(squared, 1)
                act.wait_ge(var_ready, i + 1)
                nc.scalar.activation(rstd[:, i:i + 1], rvar[:, i:i + 1], ACT.Sqrt).then_inc(rstd_ready, 1)
            highs(0)
            act.wait_ge(x_turned, TT)
            act.wait_ge(gb_ready, 1)
            for k in range(KT_D):
                nc.scalar.activation(hT_hi[:, k, :], ps[:, k, :], ACT.Copy,
                                     scale=gb[:, k:k + 1]).then_inc(hT_hi_ready, 1)

            def take_step(n):
                kind = step_kind(n)
                u, j = n // 6, n % 2
                src = ps[:, pbank(n), :]
                if kind in ("q", "v") or (kind == "k" and UNITS[u] in STACKED):
                    act.wait_ge(projected, n + 1)
                    if kind in "kq" and u:
                        act.wait_ge(scored, before_in_place(n))
                    if kind in "kq" and UNITS[u] in STACKED:
                        for e in range(2):
                            same, _ = halves(e)
                            dst = KTs[same, 2 * j + e, 0, :] if kind == "k" else QTs[same, 2 * j + e, :]
                            nc.scalar.activation(dst, src[same, :], ACT.Copy,
                                                 scale=HD ** -0.5 if kind == "q" else 1.0).then_inc(split_hi, 1)
                    elif kind == "q":
                        nc.scalar.activation(residue_major(UNITS[u], QTf[:, j, 0:SEQ]),
                                             residue_order(UNITS[u], src), ACT.Copy,
                                             scale=HD ** -0.5).then_inc(proj_taken[pbank(n)], 1)
                    else:
                        if u >= 2:
                            act.wait_ge(valued, HU * (u - 1))
                        if UNITS[u] == FULL:
                            nc.scalar.copy(split_values(u)[:, 2 * j:2 * j + 2, :, 0, :],
                                           src.rearrange("p (t h c) -> p t h c", t=2, h=HU)).then_inc(v_split_hi, 1)
                        else:
                            V = V_odd if u % 2 else V_even
                            nc.scalar.copy(V[:, 2 * j:2 * j + 2, :].rearrange("p t c -> p (t c)"),
                                           src).then_inc(proj_taken[pbank(n)], 1)
                elif kind == "z":
                    act.wait_ge(projected, n + 1)
                    nc.scalar.activation(zf[:, n - NZ0, :], src, ACT.Tanh, scale=0.5).then_inc(z_tanh, 1)
                elif kind in ("ra", "rb"):
                    act.wait_ge(projected, n + 1)
                    b = kind == "rb"
                    c = 2 * ((n - NR0) // 6) + j
                    if n < NR0 + 6:
                        act.wait_ge(turned, _t)
                    else:
                        act.wait_ge(merged, 2 * ((n - NR0) // 6))
                    nc.scalar.activation(gate[:, 2 * b + j, :], src, ACT.Tanh, scale=0.5,
                                         bias=hbias[:, 8 * b + c:8 * b + c + 1]).then_inc(proj_taken[pbank(n)], 1)

            def take_turns(h):
                for f in range(h.tfills):
                    if h.kind == FULL:
                        act.wait_ge(turned, h.t0 + f + 1)
                        act.wait_ge(valued, h.n)
                        n = P * len(h.blocks[4 * f:4 * f + 4])
                        src, dst = ps[:, TURN_BANKS[f], 0:n], turned_columns(pT_hi, f)
                        if f == 2:
                            src = src.rearrange("p (a c) -> p a c", a=2)
                        nc.scalar.copy(dst, src).then_inc(turned_hi, 1)
                    elif (h.t0 + f) % 2 == 0:
                        act.wait_ge(turned, h.t0 + f + 1)
                        if h.n:
                            act.wait_ge(valued, h.n)
                        n = P * len(h.blocks[4 * f:4 * f + 4])
                        nc.scalar.copy(probsT[:, 512 * f:512 * f + n],
                                       ps[:, TB, 0:n]).then_inc(turn_taken[0], 1)

            def exps(h, between):
                for i, (at, n) in enumerate(h.rows):
                    k = [a <= i < a + c for a, c, _ in h.minima].index(True)
                    act.wait_ge(min_ready, h.m0 + k + 1)
                    row = probs[:, h.n % 2, at:at + n]
                    nc.scalar.activation(row, row, ACT.Exp, bias=nmin(h, i), scale=-1.0,
                                         accum_out=row_sum(h, i)).then_inc(exp_ready, 1)
                    if i == 1:
                        between()

            def take_o_lows(h):
                act.wait_ge(valued, h.n + 1)
                if h.n > NDIL * HU:
                    act.wait_ge(values_taken, h.n)
                nc.scalar.copy(o_lows[:, :], ps[HD:2 * HD, PVB, :]).then_inc(o_lows_ready, 1)

            def by_position(g):
                return stats_dram.rearrange("(n p) c -> p n c" if DIL[g] == 1 else "(p n) c -> p n c", p=P)

            def store_stats(g):
                act.wait_ge(exp_ready, TT * HU * (g + 1))
                cols = slice(8 * g, 8 * g + 8)
                act.dma_start(by_position(g)[:, :, cols], stats[:, :, cols]).then_inc(stats_out, 16)

            def load_stats():
                act.wait_ge(stats_out, 16 * NDIL)
                for g in range(NDIL):
                    dst = stats3[:, TT * g:TT * g + TT, :, :].rearrange("p n g c -> p n (g c)")
                    act.dma_start(dst, by_position(g)).then_inc(stats_in, 16)

            def merged_high(n):
                d = ysteps(n)
                act.wait_ge(merged, d + 1)
                nc.scalar.copy(mrg_hi[:, d, :], ysum[:, d % 2, :]).then_inc(mrg_hi_ready, 1)

            for s in range(NS):
                if s:
                    take_step(s - 1)
                if s + 2 < NS:
                    highs(s + 2)
                if s == COEF + 1:
                    act.wait_ge(gdif_ready, 1)
                    nc.scalar.activation(gexp[:], gdif[:], ACT.Exp).then_inc(gexp_ready, 1)
                if s and step_kind(s - 1) == "y":
                    merged_high(s - 1)
                if s == 2 * OUT_AT - 3:
                    for k in range(4):
                        wo_highs(k)
                if s >= NS - 2:
                    for k in (4, 5) if s == NS - 2 else (6, 7):
                        wo_highs(k)
                for n in gated_in(s - 1):
                    _, w, c = GATED[n]
                    if n == 0:
                        act.wait_ge(misc_ready, len(MISC))
                    if w == "a":
                        act.wait_ge(dil_gated, c + 1)
                    else:
                        act.wait_ge(moba_gated, c + 1)
                    t = c if w == "a" else 2 + c
                    nc.scalar.copy(gat_hi[:, t, :], zf[:, t, :]).then_inc(gated_hi, 1)
                lows_due = s in VALUES and HEADS[VALUES[s]].kind == FULL
                if s in SCORES:
                    exps(HEADS[SCORES[s]], lambda: lows_due and take_o_lows(HEADS[VALUES[s]]))
                elif lows_due:
                    take_o_lows(HEADS[VALUES[s]])
                if s in TURNS:
                    take_turns(HEADS[TURNS[s]])
                for g in range(NDIL):
                    if s == scores_slot(HU * g + 3) + 1:
                        store_stats(g)
                if s == COEF - 1:
                    load_stats()
            merged_high(NS - 1)

            for i in range(TT):
                for g in groups_of(i):
                    _, at, n = GROUPS[g]
                    act.wait_ge(res_added, g + 1)
                    nc.scalar.activation(ps[:, OUT_BANKS[g], 0:n], res[:, i % 2, at:at + n],
                                         ACT.Square, accum_out=out_ss[:, g:g + 1]).then_inc(res_squared, 1)
                act.wait_ge(out_mean, groups_of(i)[-1] - i)
                act.wait_ge(res_squared, groups_of(i)[-1] + 1)
                nc.scalar.activation(rms[:, i:i + 1], out_ss[:, g:g + 1], ACT.Sqrt, scale=1.0 / D,
                                     bias=mean[:, g - 1:g]).then_inc(out_rms, 1)

        @block.vector
        def _(dve):
            chain = [0]

            def link(ins):
                ins.then_inc(dve_chain, 1)
                chain[0] += 1
                dve.wait_ge(dve_chain, chain[0])

            def scale_rows(i):
                dve.wait_ge(rstd_ready, i + 1)
                nc.vector.tensor_scalar(xs[:, i, :], xs[:, i, :], rstd[:, i:i + 1], None,
                                        ALU.mult).then_inc(x_scaled, 1)

            for i in range(TT):
                dve.wait_ge(squared, i + 1)
                link(nc.vector.tensor_scalar(var[:, i:i + 1], ss[:, i:i + 1], 1.0 / D, EPS, ALU.mult, ALU.add))
                nc.vector.reciprocal(rvar[:, i:i + 1], var[:, i:i + 1]).then_inc(var_ready, 1)
                scale_rows(i)
            dve.wait_ge(vecs_turned, 1)
            link(nc.vector.tensor_copy(gb[:], ps[:, 7, SEQ - 24:SEQ]))
            nc.vector.tensor_scalar(hbias[:], gb[:, 8:24], 0.5, None, ALU.mult).then_inc(gb_ready, 1)
            dve.wait_ge(hi_ready, 1)
            src, kt = raw_half(0)
            nc.vector.tensor_tensor(ring(w_lo, 0, kt), src, ring(w_hi, 0, kt).bitcast(F32),
                                    ALU.subtract).then_inc(lo_ready, 1)
            for k in range(KT_D):
                dve.wait_ge(hT_hi_ready, k + 1)
                nc.vector.scalar_tensor_tensor(out=hT_lo[:, k, :], in0=ps[:, k, :], scalar=gb[:, k:k + 1],
                                               in1=hT_hi[:, k, :].bitcast(F32), op0=ALU.mult,
                                               op1=ALU.subtract).then_inc(hT_lo_ready, 1)

            def wo_lows(k):
                dve.wait_ge(wo_hi_ready, k + 1)
                nc.vector.tensor_tensor(wo("lo", k), raw_out(k), wo("hi", k).bitcast(F32),
                                        ALU.subtract).then_inc(wo_lo_ready, 1)

            def stack_parts(n):
                src = ps[:, pbank(n), :]
                for e in range(2):
                    same, other = halves(e)
                    dve.wait_ge(split_hi, stacks_before(n) + e + 1)
                    if step_kind(n) == "q":
                        hi, lo = (QTs[rows, 2 * (n % 2) + e, :] for rows in (same, other))
                        nc.vector.scalar_tensor_tensor(out=lo, in0=src[same, :], scalar=HD ** -0.5,
                                                       in1=hi.bitcast(F32), op0=ALU.mult,
                                                       op1=ALU.subtract).then_inc(stacked, 1)
                    else:
                        k = KTs[:, 2 * (n % 2) + e, :, :]
                        nc.vector.tensor_tensor(k[same, 1, :], src[same, :], k[same, 0, :].bitcast(F32),
                                                ALU.subtract).then_inc(k_low, 1)

            def copy_parts(n):
                for e in range(2):
                    same, other = halves(e)
                    k = KTs[:, 2 * (n % 2) + e, :, :]
                    dve.wait_ge(k_low, k_stacks_before(n) + e + 1)
                    nc.vector.tensor_copy(k[other, :, :], k[same, :, :].bitcast(F32)).then_inc(stacked, 1)

            def take_step(n):
                kind, u, j = step_kind(n), n // 6, n % 2
                if kind in "kq" and UNITS[u] in STACKED:
                    stack_parts(n)
                elif kind == "v" and UNITS[u] == FULL:
                    dve.wait_ge(v_split_hi, v_steps_before(n) + 1)
                    hi, lo = (split_values(u)[:, 2 * j:2 * j + 2, :, part, :] for part in range(2))
                    nc.vector.tensor_tensor(lo, ps[:, pbank(n), :].rearrange("p (t h c) -> p t h c", t=2, h=HU),
                                            hi.bitcast(F32), ALU.subtract).then_inc(proj_taken[pbank(n)], 1)
                elif kind == "k":
                    dve.wait_ge(projected, n + 1)
                    dve.wait_ge(scored, before_in_place(n))
                    nc.vector.tensor_copy(residue_major(UNITS[u], KTf[:, j, 0:SEQ]),
                                          residue_order(UNITS[u], ps[:, pbank(n), :])).then_inc(proj_taken[pbank(n)], 1)
                elif kind == "z":
                    z = zf[:, n - NZ0, :]
                    dve.wait_ge(z_tanh, n - NZ0 + 1)
                    nc.vector.scalar_tensor_tensor(out=z, in0=z, scalar=1.0, in1=ps[:, pbank(n), :],
                                                   op0=ALU.add, op1=ALU.mult).then_inc(proj_taken[pbank(n)], 1)

            def take_misc(m, c, g):
                dve.wait_ge(misc_ready, m + 1)
                src, acc = ps[:, MB, :], dil_T[:, c, :]
                if g == 0:
                    nc.vector.tensor_copy(acc, src).then_inc(misc_taken, 1)
                else:
                    dve.wait_ge(misc_taken, m)
                    acc = residue_order(g, acc)
                    nc.vector.tensor_tensor(acc, residue_major(g, src), acc, ALU.add).then_inc(misc_taken, 1)

            def gate_dilated(c):
                m = [at for _, at in MISC].index((c, NDIL - 1))
                dve.wait_ge(misc_taken, m + 1)
                proj_taken_wait(dve, NZ0 + c)
                nc.vector.tensor_tensor(zf[:, c, :], dil_T[:, c, :], zf[:, c, :], ALU.mult).then_inc(dil_gated, 1)

            def gate_moba(c):
                dve.wait_ge(values_taken, NDIL * HU + 2 * c + 2)
                proj_taken_wait(dve, NZ0 + 2 + c)
                z = zf[:, 2 + c, :]
                nc.vector.tensor_tensor(z, o_full[:, c, :], z, ALU.mult).then_inc(moba_gated, 1)

            def recips(h):
                n = h.n - NDIL * HU
                dve.wait_ge(exp_ready, TT * (h.n + 1))
                nc.vector.reciprocal(frec[:, n, :], fsum[:, n, :]).then_inc(frec_ready, 1)

            def gated_lows(n):
                _, w, c = GATED[n]
                t = c if w == "a" else 2 + c
                dve.wait_ge(gated_hi, n + 1)
                nc.vector.tensor_tensor(gat_lo[:, t, :], zf[:, t, :], gat_hi[:, t, :].bitcast(F32),
                                        ALU.subtract).then_inc(gated_lo, 1)

            def take_turns(h):
                for f in range(h.tfills):
                    if h.kind == FULL:
                        dve.wait_ge(turned_hi, 3 * (h.n - NDIL * HU) + f + 1)
                        n = P * len(h.blocks[4 * f:4 * f + 4])
                        src = ps[:, TURN_BANKS[f], 0:n]
                        if f == 2:
                            src = src.rearrange("p (a c) -> p a c", a=2)
                        nc.vector.tensor_tensor(turned_columns(pT_lo, f), src,
                                                turned_columns(pT_hi, f).bitcast(F32),
                                                ALU.subtract).then_inc(turn_taken[f], 1)
                    elif (h.t0 + f) % 2 == 1:
                        dve.wait_ge(turned, h.t0 + f + 1)
                        if h.n:
                            dve.wait_ge(valued, h.n)
                        n = P * len(h.blocks[4 * f:4 * f + 4])
                        nc.vector.tensor_copy(probsT[:, 512 * f:512 * f + n],
                                              ps[:, TB + 1, 0:n]).then_inc(turn_taken[1], 1)

            def mask_fill(h, f):
                lo, hi, _ = h.fills[f]
                dve.wait_ge(scored, h.s0 + f + 1)
                if h.n >= 2 and f == 0:
                    last = HEADS[h.n - 2]
                    dve.wait_ge(turned, last.t0 + last.tfills)
                src = ps[:, SB + (h.s0 + f) % 2, lo:hi]
                at = pfill(h.kind, f)
                dst = probs[:, h.n % 2, at + lo:at + hi]
                if h.kind == FULL:
                    dist = d_full[:, 512 - hi:512]
                elif h.kind == BAND:
                    dist = d_band[:, lo:hi]
                else:
                    dist = (d_quad if h.kind == QUAD else d_hex)[:, :].unsqueeze(1).broadcast_to([P, TT, P])
                    dst, src = (t.rearrange("p (i c) -> p i c", i=TT) for t in (dst, src))
                nc.vector.scalar_tensor_tensor(out=dst, in0=dist, scalar=SLOPE[h.n], in1=src, op0=ALU.mult,
                                               op1=ALU.subtract).then_inc(masked, 1)

            def min_rows(h, k):
                i, n, f = h.minima[k]
                dve.wait_ge(masked, h.s0 + f + 1)
                at, w = h.rows[i]
                src = probs[:, h.n % 2, at:at + n * w].rearrange("p (i c) -> p i c", i=n)
                nc.vector.tensor_reduce(nmin(h, i, n), src, AX.X, ALU.min).then_inc(min_ready, 1)

            def softmax_in(h, between):
                k = 0
                for f in range(len(h.fills)):
                    mask_fill(h, f)
                    if f == min(1, len(h.fills) - 1):
                        between()
                    while k < len(h.minima) and h.minima[k][2] < f:
                        min_rows(h, k)
                        k += 1
                while k < len(h.minima):
                    min_rows(h, k)
                    k += 1

            def take_values(h):
                if h.unit < NDIL:
                    dve.wait_ge(valued, h.n + 1)
                    nc.vector.tensor_copy(o_dil[:, h.unit, :, HD * h.local:HD * h.local + HD],
                                          ps[:, PVB, 0:UW].rearrange("p (t c) -> p t c", t=TT)
                                          ).then_inc(values_taken, 1)
                else:
                    dve.wait_ge(o_lows_ready, h.n - NDIL * HU + 1)
                    dst = o_full[h.part:h.part + HD, (h.n - NDIL * HU) // 2, :]
                    nc.vector.tensor_tensor(dst, ps[0:HD, PVB, :], o_lows[:, :], ALU.add).then_inc(values_taken, 1)

            def coef_begin():
                dve.wait_ge(stats_in, 16 * NDIL)
                m = [stats3[:, :, g, 0:HU] for g in range(NDIL)]
                link(nc.vector.tensor_tensor(gmin[:], m[0], m[1], ALU.min))
                link(nc.vector.tensor_tensor(gmin[:], gmin[:], m[2], ALU.min))
                nc.vector.tensor_tensor(gdif[:], gmin[:].unsqueeze(2).broadcast_to([P, NDIL * TT, NDIL, HU]),
                                        stats3[:, :, :, 0:HU], ALU.subtract).then_inc(gdif_ready, 1)

            def coef_end():
                dve.wait_ge(gexp_ready, 1)
                link(nc.vector.tensor_tensor(gsum[:], gexp[:], stats3[:, :, :, HU:2 * HU], ALU.mult))
                link(nc.vector.tensor_tensor(gtot[:], gsum[:, :, 0, :], gsum[:, :, 1, :], ALU.add))
                link(nc.vector.tensor_tensor(gtot[:], gtot[:], gsum[:, :, 2, :], ALU.add))
                link(nc.vector.reciprocal(grec[:], gtot[:]))
                for g in range(NDIL):
                    r = slice(TT * g, TT * g + TT)
                    last = nc.vector.tensor_tensor(coef[:, r, :], gexp[:, r, g, :], grec[:, r, :], ALU.mult)
                    link(last)

            def scale_group(g):
                dve.wait_ge(values_taken, HU * (g + 1))
                o = o_dil[:, g, :, :].rearrange("p t (h c) -> p (t h) c", c=HD)
                c = coef[:, TT * g:TT * g + TT, :].rearrange("p t h -> p (t h)")
                nc.vector.tensor_tensor(o, o, c.unsqueeze(2).broadcast_to([P, TT * HU, HD]),
                                        ALU.mult).then_inc(o_scaled, 1)

            def merge(n):
                d, j = ysteps(n), n % 2
                dve.wait_ge(projected, n + 1)
                proj_taken_wait(dve, n - 2)
                proj_taken_wait(dve, n - 4)
                if d >= 1:
                    dve.wait_ge(mrg_hi_ready, d)
                link(nc.vector.scalar_tensor_tensor(out=ysum[:, 0, :] if d % 2 == 0 else ysum[:, 1, :],
                                                    in0=gate[:, j, :], scalar=1.0, in1=ps[:, ybank(n), :],
                                                    op0=ALU.add, op1=ALU.mult))
                g = gate[:, 2 + j, :]
                nc.vector.scalar_tensor_tensor(out=g, in0=g, scalar=1.0, in1=ps[:, ybank(n) + 1, :], op0=ALU.add,
                                               op1=ALU.mult).then_inc(y_taken, 1)
                dve.wait_ge(y_taken, d + 1)
                acc = ysum[:, d % 2, :]
                nc.vector.tensor_tensor(acc, acc, g, ALU.add).then_inc(merged, 1)
                dve.wait_ge(mrg_hi_ready, d + 1)
                nc.vector.tensor_tensor(mrg_lo[:, d, :], acc, mrg_hi[:, d, :].bitcast(F32),
                                        ALU.subtract).then_inc(mrg_lo_ready, 1)

            dve.wait_ge(consts_ready, 2)
            apart = d_hex[:].bitcast(I32)
            link(nc.vector.tensor_scalar(apart, apart, 3, None, ALU.bitwise_and))
            link(nc.vector.tensor_scalar(d_hex[:], apart, 1.0, BIG, ALU.min, ALU.mult))
            link(nc.vector.tensor_tensor(d_hex[:], d_hex[:], d_quad[:], ALU.max))
            for t in (pT_hi, pT_lo):
                link(nc.vector.tensor_scalar(t[:, T_ZERO:T_ZERO + P], ident[:], 0.0, None, ALU.mult))
            for s in range(NS):
                if s:
                    take_step(s - 1)
                if s and step_kind(s - 1) == "y":
                    merge(s - 1)
                if s == 2 * OUT_AT - 3:
                    for k in range(4):
                        wo_lows(k)
                if s >= NS - 2:
                    for k in (4, 5) if s == NS - 2 else (6, 7):
                        wo_lows(k)
                misc = [(m, at) for m, (slot, at) in enumerate(MISC) if slot == s]
                if s in SCORES:
                    softmax_in(HEADS[SCORES[s]], lambda: [take_misc(m, *at) for m, at in misc])
                else:
                    for m, at in misc:
                        take_misc(m, *at)
                if s in VALUES:
                    take_values(HEADS[VALUES[s]])
                if s in SCORES and HEADS[SCORES[s]].kind == FULL:
                    recips(HEADS[SCORES[s]])
                if s in TURNS:
                    take_turns(HEADS[TURNS[s]])
                if s and stacks(s - 1) and step_kind(s - 1) == "k":
                    copy_parts(s - 1)
                if s == COEF:
                    coef_begin()
                if s == COEF + 1:
                    coef_end()
                if COEF < s <= COEF + NDIL:
                    scale_group(s - COEF - 1)
                for n in gated_in(s):
                    _, w, c = GATED[n]
                    (gate_dilated if w == "a" else gate_moba)(c)
                for n in gated_in(s - 1):
                    gated_lows(n)
            merge(NS - 1)

            dve.wait_ge(fg_in, 16)
            for i in range(TT):
                dve.wait_ge(res_in[i % 2], 16 * (i // 2 + 1))
                groups = groups_of(i)
                for g in groups:
                    _, at, n = GROUPS[g]
                    part, cols = res[:, i % 2, at:at + n], slice(at, at + n)
                    dve.wait_ge(out_ready, g + 1)
                    nc.vector.scalar_tensor_tensor(out=part, in0=ps[:, OUT_BANKS[g], 0:n], scalar=0.25,
                                                   in1=part, op0=ALU.mult, op1=ALU.add).then_inc(res_added, 1)
                    dve.wait_ge(res_added, g + 1)
                    if g == groups[0] and i >= 2:
                        dve.wait_ge(stored[i % 2], 32)
                    nc.vector.tensor_tensor(weighted[:, i % 2, cols], part, fg[:, cols],
                                            ALU.mult).then_inc(weighed, 1)
                    if g != groups[-1]:
                        dve.wait_ge(res_squared, g + 1)
                        if g == groups[0]:
                            nc.vector.tensor_scalar(mean[:, g:g + 1], out_ss[:, g:g + 1], 1.0 / D, EPS,
                                                    ALU.mult, ALU.add).then_inc(out_mean, 1)
                        else:
                            dve.wait_ge(out_mean, g - i)
                            nc.vector.scalar_tensor_tensor(out=mean[:, g:g + 1], in0=out_ss[:, g:g + 1],
                                                           scalar=1.0 / D, in1=mean[:, g - 1:g], op0=ALU.mult,
                                                           op1=ALU.add).then_inc(out_mean, 1)
                dve.wait_ge(out_rms, i + 1)
                link(nc.vector.reciprocal(rstd[:, TT + i:TT + i + 1], rms[:, i:i + 1]))
                dve.wait_ge(weighed, groups[-1] + 1)
                for g in groups:
                    _, at, n = GROUPS[g]
                    cols = weighted[:, i % 2, at:at + n]
                    nc.vector.tensor_scalar(cols, cols, rstd[:, TT + i:TT + i + 1], None,
                                            ALU.mult).then_inc(out_done, 1)


_INS = ["x", "norm_g", "w_in", "b_merge", "w_pa", "w_pb", "w_out", "final_g"]
_FLAT = {"w_in", "w_pa", "w_pb", "w_out"}


def kernel(**inputs):
    import concourse.bacc as bacc
    from concourse.bass_utils import run_bass_kernel_spmd

    nc = bacc.Bacc("TRN2", target_bir_lowering=False, num_devices=1)
    arrays, args = {}, []
    for name in _INS:
        a = np.ascontiguousarray(inputs[name])
        if name in _FLAT:
            a = a.reshape(a.shape[1:])
        arrays[f"in_{name}"] = a
        args.append(nc.dram_tensor(f"in_{name}", a.shape, mybir.dt.from_np(a.dtype), kind="ExternalInput").ap())
    out = nc.dram_tensor("out_0", (1, SEQ, D), F32, kind="ExternalOutput").ap()
    hybrid_layer_program(nc, *args, out)
    r = run_bass_kernel_spmd(nc, [arrays], core_ids=[0])
    return r.results[0]["out_0"]
```
